# Optimizing a Trainium2 kernel written in Bass

```python
import jax, jax.numpy as jnp
from jax import lax
import numpy as np

D_MODEL = 1024
BATCH = 1
SEQ = 512
DEPTH = 2

GM_WIDTH = D_MODEL
GM_CHUNK = 128
GM_GROUPS = 8
GM_GROUP_DIM = GM_WIDTH // GM_GROUPS
ML_WIDTH = D_MODEL
ML_HEADS = 4
ML_HEAD_DIM = ML_WIDTH // ML_HEADS
ML_CHUNK = 128
ML_CONV = 5
F_BIAS_INIT = 3.0
IN_COLS = 2 * GM_WIDTH + 2 * ML_WIDTH + 2 * D_MODEL
SPLITS = [GM_WIDTH, 2 * GM_WIDTH, 2 * GM_WIDTH + ML_WIDTH, 2 * GM_WIDTH + 2 * ML_WIDTH,
          2 * GM_WIDTH + 2 * ML_WIDTH + D_MODEL]
PEER_HEADS = 8
PEER_KEYS = 128
PEER_EXPERTS = PEER_KEYS * PEER_KEYS
PEER_TOPK = 16
PEER_QDIM = 256
PEER_HALF = PEER_QDIM // 2
PEER_TOKENS = 128
EPS = 1e-6
NEG = -1e30

kernel_name = "hybrid_gmlp_mlstm_peer_encoder"

def rmsnorm(x, g):
    xf = x.astype(jnp.float32)
    y = xf * lax.rsqrt(jnp.mean(xf * xf, axis=-1, keepdims=True) + EPS)
    return (y * g.astype(jnp.float32)).astype(x.dtype)

def gmlp_spatial_gate(u, v, g_v, w_s, b_s):
    B, S, _ = v.shape
    v = rmsnorm(v, g_v).reshape(B, S // GM_CHUNK, GM_CHUNK, GM_GROUPS, GM_GROUP_DIM)
    mixed = jnp.einsum('gts,bcsgd->bctgd', w_s, v) + b_s.T[None, None, :, :, None]
    return u * mixed.reshape(B, S, GM_WIDTH)

def centred_dwconv(x, w, b):
    pad = ML_CONV // 2
    y = lax.conv_general_dilated(x, w[:, None, :], window_strides=(1,), padding=[(pad, pad)],
                                 dimension_numbers=('NWC', 'WIO', 'NWC'),
                                 feature_group_count=x.shape[-1])
    return y + b

def mlstm_chunkwise(q, k, v, log_i, log_f):
    B, H, S, dh = q.shape
    L = ML_CHUNK
    nc = S // L

    def to_chunks(a):
        return jnp.moveaxis(a.reshape((B, H, nc, L) + a.shape[3:]), 2, 0)

    xs = tuple(to_chunks(a) for a in (q, k, v, log_i, log_f))
    tri = jnp.tril(jnp.ones((L, L), dtype=bool))

    def step(carry, chunk):
        C, n, m = carry
        qt, kt, vt, it, ft = chunk
        b = jnp.cumsum(ft, axis=-1)
        d = jnp.where(tri, b[..., :, None] - b[..., None, :] + it[..., None, :], NEG)
        inter = b + m[..., None]
        m_t = jnp.maximum(inter, jnp.max(d, axis=-1))
        w_intra = jnp.exp(d - m_t[..., None])
        w_inter = jnp.exp(inter - m_t)
        s = jnp.einsum('bhtd,bhsd->bhts', qt, kt) * w_intra
        num = jnp.einsum('bhts,bhsd->bhtd', s, vt) + w_inter[..., None] * jnp.einsum('bhvk,bhtk->bhtv', C, qt)
        den = jnp.sum(s, axis=-1) + w_inter * jnp.einsum('bhk,bhtk->bht', n, qt)
        h = num / jnp.maximum(jnp.abs(den), jnp.exp(-m_t))[..., None]
        bL = b[..., -1]
        g_s = bL[..., None] - b + it
        m_new = jnp.maximum(bL + m, jnp.max(g_s, axis=-1))
        ws = jnp.exp(g_s - m_new[..., None])
        wc = jnp.exp(bL + m - m_new)
        C_new = wc[..., None, None] * C + jnp.einsum('bhs,bhsv,bhsk->bhvk', ws, vt, kt)
        n_new = wc[..., None] * n + jnp.einsum('bhs,bhsk->bhk', ws, kt)
        return (C_new, n_new, m_new), h

    init = (jnp.zeros((B, H, dh, dh), jnp.float32), jnp.zeros((B, H, dh), jnp.float32),
            jnp.zeros((B, H), jnp.float32))
    _, hs = lax.scan(step, init, xs)
    return jnp.moveaxis(hs, 0, 2).reshape(B, H, S, dh)

def mlstm_branch(xm, o_pre, conv_w, conv_b, w_q, w_k, w_v, w_gate, b_gate, head_g, skip):
    B, S, _ = xm.shape
    xc = jax.nn.silu(centred_dwconv(xm, conv_w, conv_b))
    heads = lambda a: a.reshape(B, S, ML_HEADS, ML_HEAD_DIM)
    q = jnp.einsum('bshd,hde->bhse', heads(xc), w_q).astype(jnp.float32)
    k = (jnp.einsum('bshd,hde->bhse', heads(xc), w_k) * ML_HEAD_DIM ** -0.5).astype(jnp.float32)
    v = jnp.einsum('bshd,hde->bhse', heads(xm), w_v).astype(jnp.float32)
    gates = (xc @ w_gate + b_gate).astype(jnp.float32).reshape(B, S, 4, ML_HEADS)
    i_f, f_f, i_b, f_b = jnp.transpose(gates, (2, 0, 3, 1))
    h_fwd = mlstm_chunkwise(q, k, v, i_f, jax.nn.log_sigmoid(f_f))
    flip = lambda a: jnp.flip(a, axis=2)
    h_bwd = flip(mlstm_chunkwise(flip(q), flip(k), flip(v), flip(i_b), flip(jax.nn.log_sigmoid(f_b))))
    h = h_fwd + h_bwd
    h = h * lax.rsqrt(jnp.mean(h * h, axis=-1, keepdims=True) + EPS) * head_g.astype(jnp.float32)[:, None, :]
    h = jnp.transpose(h, (0, 2, 1, 3)).reshape(B, S, ML_WIDTH).astype(xm.dtype)
    return jax.nn.sigmoid(o_pre) * (h + skip * xc)

def hybrid_mixer(h, w_in, gm_norm_g, gm_w_s, gm_b_s, ml_conv_w, ml_conv_b, ml_w_q, ml_w_k, ml_w_v,
                 ml_w_gate, ml_b_gate, ml_head_g, ml_skip, w_branch_a, w_branch_b, w_out):
    z = jnp.einsum('bsd,dc->bsc', h, w_in)
    z_u, z_v, xm, o_pre, g_a, g_b = jnp.split(z, SPLITS, axis=-1)
    y_a = gmlp_spatial_gate(jax.nn.gelu(z_u), jax.nn.gelu(z_v), gm_norm_g, gm_w_s, gm_b_s)
    y_b = mlstm_branch(xm, o_pre, ml_conv_w, ml_conv_b, ml_w_q, ml_w_k, ml_w_v, ml_w_gate, ml_b_gate,
                       ml_head_g, ml_skip)
    merged = jax.nn.sigmoid(g_a) * (y_a @ w_branch_a) + jax.nn.sigmoid(g_b) * (y_b @ w_branch_b)
    return merged @ w_out

def peer_ffn(x, w_query, sub_keys, expert_u, expert_v):
    B, S, D = x.shape
    xt = x.reshape((B * S) // PEER_TOKENS, PEER_TOKENS, D)

    def block(xb):
        n = xb.shape[0]
        q = (xb @ w_query).reshape(n, PEER_HEADS, 2, PEER_HALF)
        s = jnp.einsum('nhpc,hpkc->nhpk', q, sub_keys).astype(jnp.float32)
        sv, si = lax.top_k(s, PEER_TOPK)
        cand = (sv[:, :, 0, :, None] + sv[:, :, 1, None, :]).reshape(n, PEER_HEADS, PEER_TOPK * PEER_TOPK)
        cv, ci = lax.top_k(cand, PEER_TOPK)
        i1 = jnp.take_along_axis(si[:, :, 0], ci // PEER_TOPK, axis=-1)
        i2 = jnp.take_along_axis(si[:, :, 1], ci % PEER_TOPK, axis=-1)
        idx = i1 * PEER_KEYS + i2
        g = jax.nn.softmax(cv, axis=-1).astype(xb.dtype)
        act = jax.nn.gelu(jnp.einsum('nhkd,nd->nhk', expert_u[idx], xb))
        return jnp.einsum('nhk,nhkd->nd', g * act, expert_v[idx])

    return lax.map(block, xt).reshape(B, S, D)

def setup_inputs(seed: int = 0) -> dict:
    key = jax.random.key(seed)
    ks = iter(jax.random.split(key, 32))
    L = DEPTH

    def nrm(shape, scale):
        return jax.random.normal(next(ks), shape, jnp.float32) * scale

    gate_b = nrm((L, 4, ML_HEADS), 0.1) + jnp.array([0.0, F_BIAS_INIT, 0.0, F_BIAS_INIT], jnp.float32)[None, :, None]
    return {
        "x": nrm((BATCH, SEQ, D_MODEL), 1.0),
        "norm_mix_g": 1.0 + nrm((L, D_MODEL), 0.02),
        "w_in": nrm((L, D_MODEL, IN_COLS), D_MODEL ** -0.5),
        "gm_norm_g": 1.0 + nrm((L, GM_WIDTH), 0.02),
        "gm_w_s": nrm((L, GM_GROUPS, GM_CHUNK, GM_CHUNK), GM_CHUNK ** -0.5),
        "gm_b_s": 1.0 + nrm((L, GM_GROUPS, GM_CHUNK), 0.1),
        "ml_conv_w": nrm((L, ML_CONV, ML_WIDTH), ML_CONV ** -0.5),
        "ml_conv_b": nrm((L, ML_WIDTH), 0.02),
        "ml_w_q": nrm((L, ML_HEADS, ML_HEAD_DIM, ML_HEAD_DIM), ML_HEAD_DIM ** -0.5),
        "ml_w_k": nrm((L, ML_HEADS, ML_HEAD_DIM, ML_HEAD_DIM), ML_HEAD_DIM ** -0.5),
        "ml_w_v": nrm((L, ML_HEADS, ML_HEAD_DIM, ML_HEAD_DIM), ML_HEAD_DIM ** -0.5),
        "ml_w_gate": nrm((L, ML_WIDTH, 4 * ML_HEADS), ML_WIDTH ** -0.5),
        "ml_b_gate": gate_b.reshape(L, 4 * ML_HEADS),
        "ml_head_g": 1.0 + nrm((L, ML_HEADS, ML_HEAD_DIM), 0.02),
        "ml_skip": 1.0 + nrm((L, ML_WIDTH), 0.02),
        "w_branch_a": nrm((L, GM_WIDTH, D_MODEL), GM_WIDTH ** -0.5),
        "w_branch_b": nrm((L, ML_WIDTH, D_MODEL), ML_WIDTH ** -0.5),
        "w_out": nrm((L, D_MODEL, D_MODEL), D_MODEL ** -0.5),
        "norm_ffn_g": 1.0 + nrm((L, D_MODEL), 0.02),
        "peer_w_query": nrm((L, D_MODEL, PEER_HEADS * PEER_QDIM), D_MODEL ** -0.5),
        "peer_sub_keys": nrm((L, PEER_HEADS, 2, PEER_KEYS, PEER_HALF), PEER_HALF ** -0.5),
        "peer_u": nrm((L, PEER_EXPERTS, D_MODEL), D_MODEL ** -0.5),
        "peer_v": nrm((L, PEER_EXPERTS, D_MODEL), (PEER_HEADS * PEER_TOPK) ** -0.5),
        "final_g": 1.0 + nrm((D_MODEL,), 0.02),
    }

def reference(x, norm_mix_g, w_in, gm_norm_g, gm_w_s, gm_b_s, ml_conv_w, ml_conv_b, ml_w_q, ml_w_k,
              ml_w_v, ml_w_gate, ml_b_gate, ml_head_g, ml_skip, w_branch_a, w_branch_b, w_out,
              norm_ffn_g, peer_w_query, peer_sub_keys, peer_u, peer_v, final_g):
    for l in range(DEPTH):
        x = x + hybrid_mixer(rmsnorm(x, norm_mix_g[l]), w_in[l], gm_norm_g[l], gm_w_s[l], gm_b_s[l],
                             ml_conv_w[l], ml_conv_b[l], ml_w_q[l], ml_w_k[l], ml_w_v[l], ml_w_gate[l],
                             ml_b_gate[l], ml_head_g[l], ml_skip[l], w_branch_a[l], w_branch_b[l], w_out[l])
        x = x + peer_ffn(rmsnorm(x, norm_ffn_g[l]), peer_w_query[l], peer_sub_keys[l], peer_u[l], peer_v[l])
    return rmsnorm(x, final_g)


_drawn_inputs = setup_inputs


def setup_inputs(seed=0):
    import zlib

    import numpy as np

    out = dict(_drawn_inputs(seed))
    spreads = {}
    factors = {'gm_norm_g': 23.783,
     'ml_conv_b': 3.636,
     'ml_head_g': 27.757,
     'ml_skip': 22.507,
     'norm_ffn_g': 22.574,
     'final_g': 24.531,
     'gm_b_s': 4.525}
    for name, (base, spread) in spreads.items():
        noise = np.random.default_rng([zlib.crc32(name.encode()), seed]).standard_normal(out[name].shape)
        drawn = base * np.exp(spread * noise) if base else spread * noise
        out[name] = __import__('jax').numpy.asarray(drawn.astype(out[name].dtype))
    for name, factor in factors.items():
        out[name] = (out[name] * factor).astype(out[name].dtype)
    return out
```

```python
from contextlib import ExitStack

import concourse.bass as bass
from concourse import mybir

ALU = mybir.AluOpType
ACT = mybir.ActivationFunctionType
AX = mybir.AxisListType
F32 = mybir.dt.float32
U32 = mybir.dt.uint32

P = 128
S = 512
D = 1024
NB = S // P
NK = D // P
L = 2
NH = 4
DH = D // NH
CONV = 5
PH = 8
KEYS = 128
TOPK = 16
EPS = 1e-6
LOWEST = -3.0e38
RING = 8
SLOTS = 8
BATCH = 4
NSEL = NB * PH

(P_MIXG, P_GMG, P_CB, P_HG, P_SK) = (8 * i for i in range(5))
P_CW = 40
P_BG = P_CW + 8 * CONV
NPAR = P_BG + 4

FILLS = ([("hT", k) for k in range(NK)] + [("v", j) for j in range(NK)]
         + [("xm", j) for j in range(NK)] + [("u", j) for j in range(NK)]
         + [("vr", i) for i in range(2 * NB)] + [("mix", g) for g in range(NK)]
         + [("o", j) for j in range(NK)] + [("gates", 0)]
         + [("ga", j) for j in range(NK)] + [("gb", j) for j in range(NK)] + [("cols", 0)])
QKV = ("q0", "q1", "k0", "k1", "v0", "v1")
FILLS += [(n, 0) for n in QKV]
for _h in range(NH):
    FILLS += [(n, _h + 1) for n in QKV] if _h + 1 < NH else []
    FILLS += [("a", 2 * _h), ("a", 2 * _h + 1), ("hd", 2 * _h), ("hd", 2 * _h + 1)]
FILLS += [("b", j) for j in range(NK)] + [("wo", i) for i in range(2 * NB)]
FILLS += [("xT", k) for k in range(NK)] + [("pq", j) for j in range(2 * PH)]
FILL_NO = {name: n for n, name in enumerate(FILLS)}

TILES = ([("v", j) for j in range(NK)] + [("xm", j) for j in range(NK)] + [("u", j) for j in range(NK)]
         + [("o", j) for j in range(NK)] + [("ga", j) for j in range(NK)] + [("gb", j) for j in range(NK)]
         + [("a", j) for j in range(NK)] + [("b", j) for j in range(NK)]
         + [("wo", i) for i in range(NK)] + [("pq", j) for j in range(2 * PH)])
TILE_NO = {name: n for n, name in enumerate(TILES)}
SECTION = {"u": 0, "v": 1, "xm": 2, "o": 3, "ga": 4, "gb": 5}


class Own:

    def __init__(self, eng):
        self.eng, self.n = eng, {}

    def tell(self, ins, sem):
        ins.then_inc(sem, 1)
        self.n[sem.name] = self.n.get(sem.name, 0) + 1

    def done(self, sem):
        self.eng.wait_ge(sem, self.n[sem.name])

    def link(self, ins, sem):
        self.tell(ins, sem)
        self.done(sem)

    def forget(self, sem):
        self.n[sem.name] = 0


def build(nc, x_in, par, bs, ws, w_in, w_qkv, w_g, w_a, w_b, w_o, ffn_g, w_pq, keys, uv, fin_g, out):
    ctx = ExitStack()
    with ctx:
        arena = ctx.enter_context(nc.sbuf_tensor("arena", [P, 53200], F32))
        at = [0]

        def take(n):
            at[0] += n
            return arena[:, at[0] - n:at[0]]

        def rows(t):
            return t.rearrange("p (b d) -> p b d", b=NB)

        def chunks(t, n=NK):
            return t.rearrange("p (k t) -> p k t", k=n)

        X = rows(take(NB * D))
        R1 = take(NK * S + 16)
        R2 = take(NK * S)
        at_R3 = at[0]
        R3 = take(NK * S)
        R4 = take(NK * (S + 4))
        R5 = take(NK * S)
        at_R6 = at[0]
        R6 = take(NK * S)
        R7 = take(NK * S)
        RW = take(RING * D)
        WQKV = take(3 * 2 * DH).rearrange("p (m c e) -> p m c e", m=3, c=2)
        PW = take(3 * D)
        HR = take(NB * DH)
        G = [take(2 * S) for _ in range(5)]
        sel = take(NH * P).rearrange("p (h m) -> p h m", h=NH)
        ident = take(P)
        prm = take(NPAR)
        cols = take(64).rearrange("p (i d b h) -> p i d b h", i=2, d=2, b=NB)
        small = take(64)
        eps = small[:, 61:62]
        row0 = small[:, 60:61]
        assert at[0] <= 53200, at

        hT, xcT = chunks(R1[:, 0:NK * S]), chunks(R7)
        h_rows, v_rows, gbT = rows(R2), rows(R2), chunks(R2)
        uT, oT = chunks(R3), chunks(R5)
        xmT = R4.rearrange("p (k t) -> p k t", k=NK)
        vT, gaT = chunks(R6), chunks(R6)
        ring = RW.rearrange("p (r k c) -> p r k c", r=RING, k=NK)
        ring4 = RW.rearrange("p (q k c) -> p q k c", q=RING // 4, k=NK)
        wsT = PW[:, 0:D].rearrange("p (g t) -> p g t", g=NK)
        bsb = PW[:, D:2 * D].rearrange("p (g t) -> p g t", g=NK)
        wg = PW[:, 2 * D:3 * D].rearrange("p (k m) -> p k m", k=NK)
        qs, ks = (R1[:, i * 2 * S:(i + 1) * 2 * S].rearrange("p (c t) -> p c t", c=2) for i in range(2))
        VA = DH + 1
        vaug = [R1[:, 4 * S + i * NB * VA:4 * S + (i + 1) * NB * VA].rearrange("p (b e) -> p b e", b=NB)
                for i in range(2)]
        h_head = HR.rearrange("p (b e) -> p b e", b=NB)
        tmp = HR[:, 0:S]
        g_i, g_f, g_t, g_F, g_M = (g[0:NH].rearrange("p (d t) -> p d t", d=2) for g in G)
        junk = G[0]
        ffg = G[2]
        ss1, ss2, ss3, ss4 = (small[:, 4 * i:4 * i + 4] for i in range(4))
        den = small[:, 16:24]
        hss = small[:, 24:28]

        def attn(d, c):
            n = (NB - c) * P if d == 0 else (c + 1) * P
            off = sum((NB - i) * P for i in range(c)) if d == 0 else 10 * P + sum((i + 1) * P for i in range(c))
            return PW[:, off:off + n], (c * P if d == 0 else 0), n

        xn = rows(R2)
        xnT = chunks(R1[:, 0:NK * S])
        q_flat = arena[:, at_R3:at_R3 + 2 * PH * S]
        qT = q_flat.rearrange("p (b m t) -> p b m t", b=NB, m=2 * PH)
        q_heads = q_flat.rearrange("p (n c) -> p n c", n=NSEL)
        slot = arena[:, at_R6:at_R6 + SLOTS * 2 * D].rearrange("p (r w d) -> p r w d", r=SLOTS, w=2)
        keysT = R5[:, 0:2 * PH * KEYS].rearrange("p (m k) -> p m k", m=2 * PH)
        q_now = R5[:, 2048:2560].rearrange("p (y h t) -> p y h t", y=2, h=2)
        x_now = R5[:, 2560:3584]
        diag = R1[:, 0:2 * BATCH * P].rearrange("p (y s m) -> p y s m", y=2, s=BATCH)
        o_ = [2 * BATCH * P]

        def r1(n):
            o_[0] += n
            return R1[:, o_[0] - n:o_[0]]
        sc2 = r1(256).rearrange("p (h k) -> p h k", h=2)
        sc2r = r1(KEYS)
        cand, cand2 = r1(256), r1(256)
        onehot, picked = (r1(512).rearrange("p (h k j) -> p h k j", h=2, k=TOPK) for _ in range(2))
        iota16 = r1(16)
        sv = r1(32).rearrange("p (h k) -> p h k", h=2)
        si = r1(32).bitcast(U32).rearrange("p (h k) -> p h k", h=2)
        cv = r1(16)
        ci = r1(16).bitcast(U32)
        cab = r1(32).bitcast(U32).rearrange("p (h k) -> p h k", h=2)
        pick = r1(32).rearrange("p (h k) -> p h k", h=2)
        idx = r1(32).bitcast(U32).rearrange("p (y k) -> p y k", y=2)
        ex = r1(16)
        gate = r1(32).rearrange("p (y k) -> p y k", y=2)
        esum, ncv, rin = r1(1), r1(1), r1(1)
        dots = r1(32).rearrange("p (y k) -> p y k", y=2)
        acts = r1(32).rearrange("p (y k) -> p y k", y=2)
        wt = r1(32).rearrange("p (y k) -> p y k", y=2)
        assert o_[0] <= NK * S

        ps = [ctx.enter_context(nc.psum_tensor(f"bank{i}", [P, S], F32))[:, :] for i in range(8)]
        bank = ps[0:2]
        ps_s = ps[2:4]
        ps_a = ps[4:6]
        ps_n = ps[6:8]
        ps_v = ps[0:2]
        ps_k = ps[2:4]

        def sem(name):
            return ctx.enter_context(nc.semaphore(name))

        s_x, s_out, s_pool = sem("x_loaded"), sem("out_stored"), sem("pool_constants")
        filled = [sem(f"bank_filled{i}") for i in range(2)]
        drained = [sem(f"bank_drained{i}") for i in range(2)]
        s_par, s_ffg, s_keys = sem("params_loaded"), sem("ffn_gain_loaded"), sem("keys_loaded")
        s_w = [sem(f"weights_loaded{i}") for i in range(RING)]
        s_qkvw = sem("qkv_weights_loaded")
        s_a, s_d = sem("act_step"), sem("dve_step")
        s_sq, s_sqv, s_sqx = sem("h_squares"), sem("v_squares"), sem("x_squares")
        s_hr, s_vs, s_xr = sem("h_rows_ready"), sem("v_rows_scaled"), sem("x_rows_ready")
        s_ya, s_yb = sem("ya_ready"), sem("yb_ready")
        s_conv, s_xc = sem("conv_done"), sem("xc_ready")
        s_gin, s_nabs, s_ln = sem("gates_in"), sem("gates_negabs"), sem("gates_ln")
        s_fm, s_rows = sem("gates_stabiliser"), sem("gates_rows_ready")
        s_em = sem("gates_em_ready")
        s_afull, s_afree = sem("a_full"), sem("a_free")
        s_arg, s_exp, s_mask, s_p = sem("attn_arg"), sem("attn_exp"), sem("attn_masked"), sem("attn_ready")
        s_sfull = sem("scores_full")
        s_nfull, s_nfree = sem("num_full"), sem("num_free")
        s_hsum, s_hsq, s_hn = sem("head_summed"), sem("head_squares"), sem("head_normed")
        s_xs = sem("xc_skip")
        s_one = sem("vaug_ones")
        s_mean, s_rstd = sem("mean_square"), sem("rstd_ready")
        s_clear_last = sem("layer_end")
        s_gather = [sem(f"gathered{i}") for i in range(SLOTS)]
        s_free = sem("slots_free")
        s_idx = sem("indices_ready")
        s_dot, s_act, s_diag = sem("dots_ready"), sem("gelu_ready"), sem("diag_ready")
        s_q, s_sc = sem("query_staged"), sem("key_scores_ready")
        s_cv, s_ex = sem("top_ready"), sem("exp_ready")
        s_vfree = sem("block_added")
        s_ps = sem("peer_dve_step")
        s_vfree0, s_iota = sem("row0_set"), sem("iota_ready")
        s_fsq, s_fin = sem("final_squares"), sem("final_ready")
        s_fms, s_frs = sem("final_mean_square"), sem("final_rstd")
        first, last_ = filled[0], s_clear_last

        def is_filled(eng, *name):
            n = FILL_NO[name]
            eng.wait_ge(filled[n % 2], n // 2 + 1)
            return bank[n % 2]

        def drain(ins, *name):
            ins.then_inc(drained[FILL_NO[name] % 2], 1)

        def is_drained(eng, *name):
            n = FILL_NO[name]
            eng.wait_ge(drained[n % 2], n // 2 + 1)

        with nc.Block() as block:
            @block.sync
            def _(sp):
                sp.dma_start(X, x_in.rearrange("(b p) d -> p b d", p=P)).then_inc(s_x, 16)

            @block.gpsimd
            def _(pool):
                pool.memset(ident, 0.0).then_inc(s_pool, 1)
                pool.memset(sel, 1.0).then_inc(s_pool, 1)
                pool.wait_ge(s_pool, 2)
                pool.affine_select(out=ident, in_=ident, compare_op=ALU.not_equal, fill=1.0, base=0,
                                   pattern=[[-1, P]], channel_multiplier=1).then_inc(s_pool, 1)
                pool.affine_select(out=sel, in_=sel, compare_op=ALU.is_equal, fill=0.0, base=0,
                                   pattern=[[-1, NH], [0, P]], channel_multiplier=1).then_inc(s_pool, 1)
                pool.wait_ge(s_pool, 4)

            @block.tensor
            def _(pe):
                pe.sem_inc(s_free, SLOTS)
                pe.sem_inc(s_vfree, 1)

            @block.vector
            def _(dve):
                dve.memset(row0, 0.0).then_inc(s_vfree0, 1)
                dve.memset(eps, EPS).then_inc(s_vfree0, 1)
                dve.wait_ge(s_vfree0, 2)
                dve.wait_ge(s_x, 16)

        with nc.Fori(0, L) as l:
            with nc.Block() as block:
                @block.sync
                def _(sp):
                    lay = bass.ds(l, 1)
                    sp.dma_start(prm, par[lay].rearrange("l p c -> (l p) c")).then_inc(s_par, 16)
                    sp.dma_start(wsT, ws[lay].rearrange("l p g t -> (l p) g t")).then_inc(s_par, 16)
                    sp.dma_start(bsb, bs[lay].rearrange("l g t -> l (g t)").to_broadcast([P, D])
                                 .rearrange("p (g t) -> p g t", g=NK)).then_inc(s_par, 16)
                    sp.dma_start(wg, w_g[lay].rearrange("l p k m -> (l p) k m")).then_inc(s_par, 16)

                    def load_qkv(h):
                        if h >= 1:
                            is_filled(sp, "v1", h - 1)
                        sp.dma_start(WQKV, w_qkv[lay, h].rearrange("l p m c e -> (l p) m c e"))\
                          .then_inc(s_qkvw, 16)

                    for n, (kind, j) in enumerate(TILES):
                        if kind == "ga" and j == 0:
                            load_qkv(0)
                        if kind == "a" and j >= 2 and j % 2 == 0:
                            load_qkv(j // 2)
                        if n >= RING:
                            old, i = TILES[n - RING]
                            is_filled(sp, old, NB * (i // 4) + NB - 1 if old == "wo" else i)
                        if kind in SECTION:
                            src = w_in[lay, SECTION[kind] * NK + j]
                        elif kind == "wo":
                            src = w_o[lay, j]
                        else:
                            src = {"a": w_a, "b": w_b, "pq": w_pq}[kind][lay, j]
                        sp.dma_start(ring[:, n % RING], src.rearrange("l p k c -> (l p) k c"))\
                          .then_inc(s_w[n % RING], 16)
                        if kind == "b" and j == 0:
                            sp.wait_ge(s_hn, 1)
                            sp.dma_start(ffg, ffn_g[lay].to_broadcast([P, D])).then_inc(s_ffg, 16)
                    is_filled(sp, "b", NK - 1)
                    sp.dma_start(keysT, keys[lay].rearrange("l p m k -> (l p) m k")).then_inc(s_keys, 16)
                    sp.wait_ge(s_keys, 16)

                @block.gpsimd
                def _(pool):
                    own = Own(pool)

                    pool.memset(xmT[:, :, 0:2], 0.0).then_inc(s_one, 1)
                    pool.memset(xmT[:, :, S + 2:S + 4], 0.0).then_inc(s_one, 1)
                    is_filled(pool, "gb", NK - 1)
                    for i in range(2):
                        pool.memset(vaug[i][:, :, DH:VA], 1.0).then_inc(s_one, 1)
                    for h in range(NH):
                        for c in range(NB):
                            for d in range(2):
                                w, t0, n = attn(d, c)
                                o = 0 if d == 0 else c * P
                                sgn = 1 if d == 0 else -1
                                pool.wait_ge(s_exp, 8 * h + 2 * c + d + 1)
                                pool.affine_select(out=w[:, o:o + P], in_=w[:, o:o + P], compare_op=ALU.is_ge,
                                                   fill=0.0, base=0, pattern=[[sgn, P]],
                                                   channel_multiplier=-sgn).then_inc(s_mask, 1)

                @block.scalar
                def _(act):
                    own = Own(act)

                    def rstd(ss, n):
                        own.link(act.activation(ss, ss, ACT.Ln, bias=eps, scale=1.0 / n), s_mean)
                        act.activation(ss, ss, ACT.Exp, scale=-0.5).then_inc(s_rstd, 1)

                    for b in range(NB):
                        act.activation(h_rows[:, b], X[:, b], ACT.Square, accum_out=ss1[:, b:b + 1])\
                           .then_inc(s_sq, 1)
                    act.wait_ge(s_sq, NB)
                    rstd(ss1, D)
                    act.wait_ge(s_par, 64)
                    for k in range(NK):
                        z = is_filled(act, "hT", k)
                        drain(act.activation(hT[:, k], z[:, :], ACT.Copy,
                                             scale=prm[:, P_MIXG + k:P_MIXG + k + 1]), "hT", k)
                    for j in range(NK):
                        drain(act.activation(vT[:, j], is_filled(act, "v", j)[:, :], ACT.Gelu_apprx_tanh), "v", j)
                    for j in range(NK):
                        drain(act.activation(xmT[:, j, 2:S + 2], is_filled(act, "xm", j)[:, :], ACT.Copy), "xm", j)
                    for j in range(NK):
                        drain(act.activation(uT[:, j], is_filled(act, "u", j)[:, :], ACT.Gelu_apprx_tanh), "u", j)
                    for b in range(NB):
                        is_drained(act, "vr", 2 * b)
                        is_drained(act, "vr", 2 * b + 1)
                        if b:
                            act.wait_ge(s_sqv, b)
                        act.activation(R5[:, 0:D], v_rows[:, b], ACT.Square, accum_out=ss2[:, b:b + 1])\
                           .then_inc(s_sqv, 1)
                    act.wait_ge(s_sqv, NB)
                    rstd(ss2, D)
                    for j in range(NK):
                        act.wait_ge(s_conv, j + 1)
                        act.activation(xcT[:, j], xcT[:, j], ACT.Silu).then_inc(s_xc, 1)
                    for j in range(NK):
                        drain(act.activation(oT[:, j], is_filled(act, "o", j)[:, :], ACT.Sigmoid), "o", j)
                    z = is_filled(act, "gates", 0)
                    for i, (g, d) in enumerate(((g_i, 0), (g_f, 0), (g_i, 1), (g_f, 1))):
                        ins = act.activation(g[:, d], z[32 * i:32 * i + NH, :], ACT.Identity,
                                             bias=prm[0:NH, P_BG + i:P_BG + i + 1])
                        if i < 3:
                            ins.then_inc(s_gin, 1)
                        else:
                            drain(ins, "gates", 0)
                    act.wait_ge(s_nabs, 1)
                    act.activation(g_t, g_t, ACT.Exp).then_inc(s_a, 1)
                    act.wait_ge(s_a, 1)
                    act.activation(g_t, g_t, ACT.Ln, bias=1.0).then_inc(s_ln, 1)
                    for j in range(NK):
                        drain(act.activation(gaT[:, j], is_filled(act, "ga", j)[:, :], ACT.Sigmoid), "ga", j)
                    for j in range(NK):
                        drain(act.activation(gbT[:, j], is_filled(act, "gb", j)[:, :], ACT.Sigmoid), "gb", j)
                    act.wait_ge(s_fm, 1)
                    act.activation(g_t, g_t, ACT.Exp, scale=-1.0).then_inc(s_em, 1)

                    def evacuate_qkv(h):
                        for e in range(2):
                            drain(act.activation(qs[:, e], is_filled(act, f"q{e}", h)[:, :], ACT.Copy), f"q{e}", h)
                        for e in range(2):
                            drain(act.activation(ks[:, e], is_filled(act, f"k{e}", h)[:, :], ACT.Copy,
                                                 scale=float(DH) ** -0.5), f"k{e}", h)
                        for i in range(2):
                            z = is_filled(act, f"v{i}", h)
                            drain(act.activation(vaug[h % 2][:, 2 * i:2 * i + 2, 0:DH],
                                                 z.rearrange("p (b e) -> p b e", b=2), ACT.Copy), f"v{i}", h)
                    evacuate_qkv(0)
                    for h in range(NH):
                        for c in range(NB):
                            for d in range(2):
                                w, t0, n = attn(d, c)
                                act.wait_ge(s_arg, 8 * h + 2 * c + d + 1)
                                act.activation(w, w, ACT.Exp).then_inc(s_exp, 1)
                        if h + 1 < NH:
                            evacuate_qkv(h + 1)
                        for e in range(2):
                            f = 2 * h + e
                            act.activation(xcT[:, f], xcT[:, f], ACT.Copy,
                                           scale=prm[:, P_SK + f:P_SK + f + 1]).then_inc(s_xs, 1)
                        act.wait_ge(s_hsum, NB * (h + 1))
                        for b in range(NB):
                            if h or b:
                                act.wait_ge(s_hsq, NB * h + b)
                            act.activation(junk[:, 0:DH], h_head[:, b], ACT.Square,
                                           accum_out=hss[:, b:b + 1]).then_inc(s_hsq, 1)
                        act.wait_ge(s_hsq, NB * (h + 1))
                        rstd(hss, DH)
                    for b in range(NB):
                        is_drained(act, "wo", b)
                        is_drained(act, "wo", NB + b)
                        if b:
                            act.wait_ge(s_sqx, b)
                        act.activation(R3[:, 0:D], X[:, b], ACT.Square, accum_out=ss3[:, b:b + 1])\
                           .then_inc(s_sqx, 1)
                    act.wait_ge(s_sqx, NB)
                    rstd(ss3, D)
                    for k in range(NK):
                        drain(act.activation(xnT[:, k], is_filled(act, "xT", k)[:, :], ACT.Copy), "xT", k)
                    for j in range(2 * PH):
                        z = is_filled(act, "pq", j)
                        drain(act.activation(qT[:, :, j], z.rearrange("p (b t) -> p b t", b=NB), ACT.Copy), "pq", j)

                @block.vector
                def _(dve):
                    own = Own(dve)

                    for b in range(NB):
                        dve.wait_ge(s_rstd, 1)
                        dve.tensor_scalar(h_rows[:, b], X[:, b], ss1[:, b:b + 1], None, ALU.mult)\
                           .then_inc(s_hr, 1)
                    dve.wait_ge(s_par, 64)
                    dve.wait_ge(s_one, 2)
                    for j in range(NK):
                        is_drained(dve, "xm", j)
                        cw = prm[:, P_CW + CONV * j:P_CW + CONV * (j + 1)]
                        own.link(dve.tensor_scalar(xcT[:, j], xmT[:, j, 0:S], cw[:, 0:1],
                                                   prm[:, P_CB + j:P_CB + j + 1], ALU.mult, ALU.add), s_d)
                        for w in range(1, CONV):
                            ins = dve.scalar_tensor_tensor(xcT[:, j], xmT[:, j, w:w + S], cw[:, w:w + 1],
                                                           xcT[:, j], ALU.mult, ALU.add)
                            if w < CONV - 1:
                                own.link(ins, s_d)
                            else:
                                ins.then_inc(s_conv, 1)
                    for i in range(2 * NB):
                        b, half = i // 2, i % 2
                        drain(dve.tensor_copy(v_rows[:, b, half * S:(half + 1) * S], is_filled(dve, "vr", i)[:, :]),
                              "vr", i)
                    for b in range(NB):
                        dve.wait_ge(s_rstd, 2)
                        dve.tensor_scalar(v_rows[:, b], v_rows[:, b], ss2[:, b:b + 1], None, ALU.mult)\
                           .then_inc(s_vs, 1)
                    for g in range(NK):
                        z = is_filled(dve, "mix", g)
                        if g:
                            dve.wait_ge(s_ya, g)
                        t3 = tmp.rearrange("p (b t) -> p b t", b=NB)
                        drain(dve.scalar_tensor_tensor(t3, z.rearrange("p (b t) -> p b t", b=NB),
                                                       prm[:, P_GMG + g:P_GMG + g + 1],
                                                       bsb[:, g].unsqueeze(1).to_broadcast([P, NB, P]),
                                                       ALU.mult, ALU.add), "mix", g)
                        is_drained(dve, "mix", g)
                        is_drained(dve, "u", g)
                        dve.tensor_tensor(uT[:, g], tmp, uT[:, g], ALU.mult).then_inc(s_ya, 1)
                    is_drained(dve, "gates", 0)
                    dve.wait_ge(s_gin, 3)
                    dve.scalar_tensor_tensor(g_t, g_f, -1.0, g_f, ALU.mult, ALU.min).then_inc(s_nabs, 1)
                    dve.wait_ge(s_ln, 1)
                    own.link(dve.scalar_tensor_tensor(g_f, g_f, 0.0, g_t, ALU.min, ALU.subtract), s_d)
                    way = (slice(None), slice(None, None, -1))
                    for d in range(2):
                        own.link(dve.tensor_tensor_scan(g_F[:, d, way[d]], g_f[:, d, way[d]], g_f[:, d, way[d]],
                                                        0.0, ALU.add, ALU.bypass), s_d)
                    own.link(dve.tensor_tensor(g_i, g_i, g_F, ALU.subtract), s_d)
                    for d in range(2):
                        own.link(dve.tensor_tensor_scan(g_M[:, d, way[d]], g_i[:, d, way[d]], g_i[:, d, way[d]],
                                                        0.0, ALU.max, ALU.max), s_d)
                    dve.tensor_tensor(g_t, g_F, g_M, ALU.add).then_inc(s_fm, 1)
                    dve.tensor_scalar(g_f, g_M, -1.0, None, ALU.mult).then_inc(s_rows, 1)
                    z = is_filled(dve, "cols", 0)
                    drain(dve.tensor_copy(cols.rearrange("p i d b h -> p (i d b h)"), z[:, 0:64]), "cols", 0)
                    is_drained(dve, "cols", 0)

                    for h in range(NH):
                        dve.wait_ge(s_afull, h + 1)
                        for c in range(NB):
                            for d in range(2):
                                w, t0, n = attn(d, c)
                                ins = dve.tensor_scalar(w, ps_a[d][:, t0:t0 + n], cols[:, 0, d, c, h:h + 1], 0.0,
                                                        ALU.add, ALU.min)
                                ins.then_inc(s_arg, 1)
                        for c in range(NB):
                            dve.wait_ge(s_sfull, NB * h + c + 1)
                            for d in range(2):
                                w, t0, n = attn(d, c)
                                dve.wait_ge(s_mask, 8 * h + 2 * c + d + 1)
                                dve.tensor_tensor(w, w, ps_s[c % 2][:, t0:t0 + n], ALU.mult).then_inc(s_p, 1)
                        for e in range(2):
                            j = 2 * h + e
                            z = is_filled(dve, "a", j)
                            drain(dve.tensor_tensor(gaT[:, j], z[:, :], gaT[:, j], ALU.mult), "a", j)
                        for i in range(2 * NB):
                            d, b = i // NB, i % NB
                            dve.wait_ge(s_nfull, 8 * h + i + 1)
                            n_ = ps_n[i % 2]
                            own.link(dve.tensor_scalar(den[:, i:i + 1], n_[:, DH:VA], -1.0,
                                                       cols[:, 1, d, b, h:h + 1], ALU.mult, ALU.max), s_d)
                            own.link(dve.tensor_tensor(den[:, i:i + 1], den[:, i:i + 1], n_[:, DH:VA], ALU.max), s_d)
                            own.link(dve.reciprocal(den[:, i:i + 1], den[:, i:i + 1]), s_d)
                            if d == 0:
                                own.link(dve.tensor_scalar(h_head[:, b], n_[:, 0:DH], den[:, i:i + 1], None,
                                                           ALU.mult), s_nfree)
                            else:
                                dve.wait_ge(s_nfree, 4 * h + 4)
                                own.link(dve.scalar_tensor_tensor(h_head[:, b], n_[:, 0:DH], den[:, i:i + 1],
                                                                  h_head[:, b], ALU.mult, ALU.add), s_hsum)
                        dve.wait_ge(s_rstd, 3 + h)
                        dve.tensor_tensor(h_head, h_head, hss.unsqueeze(2).to_broadcast([P, NB, DH]),
                                          ALU.mult).then_inc(s_hn, 1)
                        for e in range(2):
                            f = 2 * h + e
                            z = is_filled(dve, "hd", f)
                            dve.wait_ge(s_xs, f + 1)
                            drain(dve.scalar_tensor_tensor(xcT[:, f], z[:, :], prm[:, P_HG + f:P_HG + f + 1],
                                                           xcT[:, f], ALU.mult, ALU.add), "hd", f)
                            is_drained(dve, "hd", f)
                            dve.tensor_tensor(oT[:, f], oT[:, f], xcT[:, f], ALU.mult).then_inc(s_yb, 1)
                    for j in range(NK):
                        z = is_filled(dve, "b", j)
                        drain(dve.tensor_tensor(gbT[:, j], z[:, :], gbT[:, j], ALU.mult), "b", j)
                        is_drained(dve, "b", j)
                        dve.tensor_tensor(gaT[:, j], gaT[:, j], gbT[:, j], ALU.add).then_inc(s_ya, 1)
                    for i in range(2 * NB):
                        half, b = i // NB, i % NB
                        z = is_filled(dve, "wo", i)
                        xs = X[:, b, half * S:(half + 1) * S]
                        drain(dve.tensor_tensor(xs, xs, z[:, :], ALU.add), "wo", i)
                    dve.wait_ge(s_ffg, 16)
                    for b in range(NB):
                        dve.wait_ge(s_rstd, 3 + NH)
                        dve.scalar_tensor_tensor(xn[:, b], X[:, b], ss3[:, b:b + 1], ffg, ALU.mult, ALU.mult)\
                           .then_inc(s_xr, 1)

                @block.tensor
                def _(pe):
                    pe.wait_ge(s_pool, 4)

                    def fill(*name):
                        n = FILL_NO[name]
                        if n >= 2:
                            pe.wait_ge(drained[n % 2], n // 2)
                        return bank[n % 2]

                    def full(ins, *name):
                        ins.then_inc(filled[FILL_NO[name] % 2], 1)

                    def tile_in(*name):
                        n = TILE_NO[name]
                        pe.wait_ge(s_w[n % RING], 16 * (n // RING + 1))
                        return ring[:, n % RING]

                    def product(kind, j, srcT):
                        z, w = fill(kind, j), tile_in(kind, j)
                        for k in range(NK):
                            ins = pe.matmul(z[:, :], w[:, k], srcT[:, k], start=(k == 0), stop=(k == NK - 1))
                        full(ins, kind, j)

                    def turn(name, i, parts):
                        z = fill(name, i)
                        for m, part in enumerate(parts):
                            ins = pe.transpose(z[:, m * P:(m + 1) * P], part, ident)
                        full(ins, name, i)

                    pe.wait_ge(s_hr, NB)
                    for k in range(NK):
                        turn("hT", k, [h_rows[:, b, k * P:(k + 1) * P] for b in range(NB)])
                    is_drained(pe, "hT", NK - 2)
                    is_drained(pe, "hT", NK - 1)
                    for kind in ("v", "xm", "u"):
                        for j in range(NK):
                            product(kind, j, hT)
                    for i in range(2 * NB):
                        b, half = i // 2, i % 2
                        turn("vr", i, [vT[:, 4 * half + m, b * P:(b + 1) * P] for m in range(4)])
                    pe.wait_ge(s_vs, NB)
                    pe.wait_ge(s_par, 64)
                    for g in range(NK):
                        z = fill("mix", g)
                        for b in range(NB):
                            ins = pe.matmul(z[:, b * P:(b + 1) * P], v_rows[:, b, g * P:(g + 1) * P], wsT[:, g],
                                            start=True, stop=True)
                        full(ins, "mix", g)
                    for j in range(NK):
                        product("o", j, hT)
                    pe.wait_ge(s_xc, NK)
                    z = fill("gates", 0)
                    for k in range(NK):
                        ins = pe.matmul(z[:, :], wg[:, k], xcT[:, k], start=(k == 0), stop=(k == NK - 1))
                    full(ins, "gates", 0)
                    for kind in ("ga", "gb"):
                        for j in range(NK):
                            product(kind, j, hT)
                    z = fill("cols", 0)
                    pe.wait_ge(s_rows, 1)
                    pe.wait_ge(s_em, 1)
                    for i, g in enumerate((g_i, g_t)):
                        for d in range(2):
                            for b in range(NB):
                                o = ((i * 2 + d) * NB + b) * NH
                                ins = pe.transpose(z[:, o:o + NH], g[:, d, b * P:(b + 1) * P], ident[0:NH, 0:NH])
                    full(ins, "cols", 0)

                    def qkv(h):
                        pe.wait_ge(s_qkvw, 16 * (h + 1))
                        for m, (w, dst) in enumerate((("q", qs), ("k", ks))):
                            for e in range(2):
                                z = fill(f"{w}{e}", h)
                                for c in range(2):
                                    ins = pe.matmul(z[:, :], WQKV[:, m, c, e * P:(e + 1) * P], xcT[:, 2 * h + c],
                                                    start=(c == 0), stop=(c == 1))
                                full(ins, f"{w}{e}", h)
                        for i in range(2):
                            z = fill(f"v{i}", h)
                            for b in range(2):
                                t0 = 2 + (2 * i + b) * P
                                for c in range(2):
                                    ins = pe.matmul(z[:, b * DH:(b + 1) * DH], xmT[:, 2 * h + c, t0:t0 + P],
                                                    WQKV[:, 2, c, :], start=(c == 0), stop=(c == 1))
                            full(ins, f"v{i}", h)

                    qkv(0)
                    pe.wait_ge(s_one, 4)
                    for h in range(NH):
                        if h:
                            pe.wait_ge(s_arg, 8 * h)
                        for d in range(2):
                            ins = pe.matmul(ps_a[d][:, :], sel[0:NH, h], g_f[:, d], start=True, stop=True)
                        ins.then_inc(s_afull, 1)
                        for n in ("q0", "q1", "k0", "k1", "v0", "v1"):
                            is_drained(pe, n, h)
                        for c in range(NB):
                            i = NB * h + c
                            if i >= 2:
                                pe.wait_ge(s_p, 2 * (i - 1))
                            for e in range(2):
                                ins = pe.matmul(ps_s[c % 2][:, :], ks[:, e, c * P:(c + 1) * P], qs[:, e],
                                                start=(e == 0), stop=(e == 1))
                            ins.then_inc(s_sfull, 1)
                        if h + 1 < NH:
                            qkv(h + 1)
                        if h == 0:
                            pe.wait_ge(s_ya, NK)
                        product("a", 2 * h, uT)
                        product("a", 2 * h + 1, uT)
                        pe.wait_ge(s_p, 8 * (h + 1))
                        for i in range(2 * NB):
                            d, b = i // NB, i % NB
                            if i in (0, 1):
                                if h:
                                    pe.wait_ge(s_hsum, 4 * h - 1 + i)
                            elif i < 6:
                                pe.wait_ge(s_nfree, 4 * h + i - 1)
                            else:
                                pe.wait_ge(s_hsum, 4 * h + i - 5)
                            srcs = range(0, b + 1) if d == 0 else range(b, NB)
                            for c in srcs:
                                w, t0, n = attn(d, c)
                                ins = pe.matmul(ps_n[i % 2][:, 0:VA], w[:, b * P - t0:(b + 1) * P - t0],
                                                vaug[h % 2][:, c], start=(c == srcs[0]), stop=(c == srcs[-1]))
                            ins.then_inc(s_nfull, 1)
                        pe.wait_ge(s_hn, h + 1)
                        for e in range(2):
                            turn("hd", 2 * h + e, [h_head[:, b, e * P:(e + 1) * P] for b in range(NB)])
                    pe.wait_ge(s_yb, NK)
                    for j in range(NK):
                        product("b", j, oT)
                    pe.wait_ge(s_ya, 2 * NK)
                    for half in range(2):
                        n0 = TILE_NO[("wo", 4 * half)]
                        for m in range(4):
                            pe.wait_ge(s_w[(n0 + m) % RING], 16 * ((n0 + m) // RING + 1))
                        w = ring4[:, (n0 % RING) // 4]
                        for b in range(NB):
                            z = fill("wo", NB * half + b)
                            for k in range(NK):
                                ins = pe.matmul(z[:, :], gaT[:, k, b * P:(b + 1) * P], w[:, k],
                                                start=(k == 0), stop=(k == NK - 1))
                            full(ins, "wo", NB * half + b)
                    pe.wait_ge(s_xr, NB)
                    for k in range(NK):
                        turn("xT", k, [xn[:, b, k * P:(k + 1) * P] for b in range(NB)])
                    is_drained(pe, "xT", NK - 2)
                    is_drained(pe, "xT", NK - 1)
                    for j in range(2 * PH):
                        product("pq", j, xnT)
                    is_drained(pe, "pq", 2 * PH - 2)
                    is_drained(pe, "pq", 2 * PH - 1)

            with nc.Block() as block:
                def numbers(b, hp, y):
                    n = b * PH + hp * 2 + y
                    return n, l * NSEL + n

                @block.gpsimd
                def _(pool):
                    pool.iota(iota16, [[1, TOPK]], base=0, channel_multiplier=0,
                              allow_small_or_imprecise_dtypes=True).then_inc(s_iota, 1)
                    want_free, want_idx = pool.alloc_register("want_free"), pool.alloc_register("want_idx")
                    pool.reg_mov(want_free, l * (NSEL * TOPK) + 1)
                    pool.reg_mov(want_idx, l * (NSEL + 1) + 1)
                    with pool.Fori(0, NSEL // 2) as pair:
                        for y in range(2):
                            pool.wait_ge(s_idx, want_idx)
                            pool.reg_add(want_idx, want_idx, 1)
                            for k in range(TOPK):
                                pool.wait_ge(s_free, want_free)
                                pool.reg_add(want_free, want_free, 1)
                                pool.indirect_dma_start(
                                    out=slot[:, k % SLOTS].rearrange("p w d -> p (w d)"), out_offset=None, in_=uv,
                                    in_offset=bass.IndirectOffsetOnAxis(ap=idx[:, y, k:k + 1], axis=0))\
                                    .then_inc(s_gather[k % SLOTS], 16)

                @block.scalar
                def _(act):
                    def stage(m, y, before):
                        if before is not None:
                            act.wait_ge(s_sc, before)
                        act.activation(q_now[:, y].rearrange("p h t -> p (h t)"), q_heads[:, m], ACT.Copy)\
                           .then_inc(s_q, 1)

                    def exps(count):
                        act.wait_ge(s_cv, count)
                        act.activation(ex, cv, ACT.Exp, bias=ncv, accum_out=esum).then_inc(s_ex, 1)

                    sel0 = l * (NSEL + 2)
                    for m in range(2):
                        stage(m, m, None)
                        exps(sel0 + m + 1)
                    with act.Fori(0, NB) as b:
                        with act.Fori(0, PH // 2) as hp:
                            for y in range(2):
                                n, N = numbers(b, hp, y)
                                stage((n + 2) % NSEL, y, sel0 + n + 1)
                                for q in range(4):
                                    act.wait_ge(s_dot, N * 4 + q + 1)
                                    act.activation(acts[:, y, 4 * q:4 * q + 4], dots[:, y, 4 * q:4 * q + 4],
                                                   ACT.Gelu_apprx_tanh).then_inc(s_act, 1)
                                exps(sel0 + n + 3)

                @block.tensor
                def _(pe):
                    sel0 = l * (NSEL + 2)

                    def key_scores(y, head, staged, copied):
                        if copied is not None:
                            pe.wait_ge(s_cv, copied)
                        pe.wait_ge(s_q, staged)
                        for h in range(2):
                            ins = pe.matmul(ps_k[y][:, h * KEYS:(h + 1) * KEYS], q_now[:, y, h],
                                            keysT[:, head * 2 + h], start=True, stop=True)
                        ins.then_inc(s_sc, 1)

                    for m in range(2):
                        key_scores(m, m, sel0 + m + 1, None)
                    with pe.Fori(0, NB) as b:
                        pe.wait_ge(s_vfree, l * NB + b + 1)
                        for half in range(2):
                            pe.matmul(ps_v[half], ident, X[:, b, half * S:(half + 1) * S], start=True, stop=False,
                                      skip_group_check=True)
                        with pe.Fori(0, PH // 2) as hp:
                            for y in range(2):
                                n, N = numbers(b, hp, y)
                                key_scores(y, (hp * 2 + y + 2) % PH, sel0 + n + 3, sel0 + n + 1)
                                for q in range(4):
                                    pe.wait_ge(s_diag, N * 4 + q + 1)
                                    for k in range(4):
                                        for half in range(2):
                                            ins = pe.matmul(ps_v[half], diag[:, q % 2, k],
                                                            slot[:, (4 * q + k) % SLOTS, 1, half * S:(half + 1) * S],
                                                            start=False, stop=False, skip_group_check=True)
                                        ins.then_inc(s_free, 1)

                @block.vector
                def _(dve):
                    own = Own(dve)

                    def step(ins):
                        own.link(ins, s_ps)

                    def top16(values, rest, best, where):
                        step(dve.max(best[:, 0:8], values))
                        step(dve.max_index(where[:, 0:8], best[:, 0:8], values))
                        step(dve.match_replace(rest, best[:, 0:8], values, LOWEST))
                        step(dve.max(best[:, 8:16], rest))
                        step(dve.max_index(where[:, 8:16], best[:, 8:16], rest))

                    def choose_first(y, scored):
                        dve.wait_ge(s_sc, scored)
                        step(dve.tensor_copy(sc2.rearrange("p h k -> p (h k)"), ps_k[y][:, 0:2 * KEYS]))
                        top16(sc2[:, 0], sc2r, sv[:, 0], si[:, 0])

                    def choose_second():
                        top16(sc2[:, 1], sc2r, sv[:, 1], si[:, 1])
                        step(dve.tensor_tensor(cand.rearrange("p (i j) -> p i j", i=TOPK),
                                               sv[:, 0].unsqueeze(2).to_broadcast([P, TOPK, TOPK]),
                                               sv[:, 1].unsqueeze(1).to_broadcast([P, TOPK, TOPK]), ALU.add))

                    def choose_pairs():
                        top16(cand, cand2, cv, ci)
                        dve.tensor_scalar(ncv, cv[:, 0:1], -1.0, None, ALU.mult).then_inc(s_cv, 1)

                    def find_rows(y):
                        step(dve.tensor_scalar(cab[:, 0], ci, 4, None, ALU.logical_shift_right))
                        step(dve.tensor_scalar(cab[:, 1], ci, TOPK - 1, None, ALU.bitwise_and))
                        full4 = [P, 2, TOPK, TOPK]
                        for h in range(2):
                            step(dve.tensor_tensor(onehot[:, h], iota16.unsqueeze(1).to_broadcast(full4[:1] + full4[2:]),
                                                   cab[:, h].unsqueeze(2).to_broadcast(full4[:1] + full4[2:]),
                                                   ALU.is_equal))
                        step(dve.tensor_tensor(picked, onehot, si.unsqueeze(2).to_broadcast(full4), ALU.mult))
                        step(dve.tensor_reduce(pick.rearrange("p h k -> p (h k)"),
                                               picked.rearrange("p h k j -> p (h k) j"), AX.X, ALU.add))
                        step(dve.tensor_scalar(pick[:, 0], pick[:, 0], float(KEYS), row0, ALU.mult, ALU.add))
                        dve.tensor_tensor(idx[:, y], pick[:, 0], pick[:, 1], ALU.add).then_inc(s_idx, 1)

                    def set_gate(y, exped):
                        dve.wait_ge(s_ex, exped)
                        step(dve.tensor_copy(rin, esum))
                        step(dve.reciprocal(rin, rin))
                        step(dve.tensor_scalar(gate[:, y], ex, rin, None, ALU.mult))

                    def next_round():
                        own.done(s_ps)
                        dve.sem_clear(s_ps)
                        own.forget(s_ps)

                    sel0 = l * (NSEL + 2)
                    dve.wait_ge(s_iota, l + 1)
                    choose_first(0, sel0 + 1)
                    choose_second()
                    choose_pairs()
                    find_rows(0)
                    set_gate(0, sel0 + 1)
                    choose_first(1, sel0 + 2)
                    choose_second()
                    choose_pairs()
                    next_round()
                    with dve.Fori(0, NB) as b:
                        step(dve.tensor_copy(x_now, xn[:, b]))
                        next_round()
                        with dve.Fori(0, PH // 2) as hp:
                            for y in range(2):
                                n, N = numbers(b, hp, y)
                                for q in range(4):
                                    for k in range(4):
                                        r = (4 * q + k) % SLOTS
                                        dve.wait_ge(s_gather[r], N * 32 + 16 * (q // 2) + 16)
                                        ins = dve.tensor_tensor_reduce(slot[:, r, 0], slot[:, r, 0], x_now, 1.0, 0.0,
                                                                       ALU.mult, ALU.add,
                                                                       dots[:, y, 4 * q + k:4 * q + k + 1])
                                    ins.then_inc(s_dot, 1)
                                    if q == 0:
                                        find_rows(1 - y)
                                    elif q == 1:
                                        set_gate(1 - y, sel0 + n + 2)
                                        choose_first(y, sel0 + n + 3)
                                    elif q == 2:
                                        choose_second()
                                    else:
                                        choose_pairs()
                                    dve.wait_ge(s_act, N * 4 + q + 1)
                                    sl = slice(4 * q, 4 * q + 4)
                                    step(dve.tensor_tensor(wt[:, y, sl], acts[:, y, sl], gate[:, y, sl], ALU.mult))
                                    dve.wait_ge(s_free, N * 16 + 4 * q + 4)
                                    dve.tensor_tensor(diag[:, q % 2],
                                                      ident.unsqueeze(1).to_broadcast([P, BATCH, P]),
                                                      wt[:, y, sl].unsqueeze(2).to_broadcast([P, BATCH, P]),
                                                      ALU.mult).then_inc(s_diag, 1)
                            next_round()
                        dve.wait_ge(s_free, (l * NB + b) * (PH * TOPK) + PH * TOPK + SLOTS)
                        step(dve.tensor_copy(X[:, b, 0:S], ps_v[0]))
                        dve.tensor_copy(X[:, b, S:D], ps_v[1]).then_inc(s_vfree, 1)
                        next_round()
                    dve.wait_ge(s_vfree, l * NB + NB + 1)
                    step(dve.tensor_scalar(row0, row0, float(KEYS * KEYS), None, ALU.add))
                    next_round()

            nc.all_engine_barrier()
            with nc.Block() as block:
                @block.sync
                def _(sp):
                    lo, hi = filled[0].num, s_clear_last.num
                    sp.sem_clear(range(lo, hi + 1))

        with nc.Block() as block:
            @block.sync
            def _(sp):
                sp.dma_start(ffg, fin_g.to_broadcast([P, D])).then_inc(s_x, 16)
                for b in range(NB):
                    sp.wait_ge(s_fin, b + 1)
                    sp.dma_start(out[b * P:(b + 1) * P, :], xn[:, b]).then_inc(s_out, 16)
                sp.wait_ge(s_out, 16 * NB)

            @block.scalar
            def _(act):
                for b in range(NB):
                    act.activation(h_rows[:, b], X[:, b], ACT.Square, accum_out=ss4[:, b:b + 1]).then_inc(s_fsq, 1)
                act.wait_ge(s_fsq, NB)
                act.activation(ss4, ss4, ACT.Ln, bias=eps, scale=1.0 / D).then_inc(s_fms, 1)
                act.wait_ge(s_fms, 1)
                act.activation(ss4, ss4, ACT.Exp, scale=-0.5).then_inc(s_frs, 1)

            @block.vector
            def _(dve):
                dve.wait_ge(s_x, 32)
                for b in range(NB):
                    dve.wait_ge(s_frs, 1)
                    dve.scalar_tensor_tensor(xn[:, b], X[:, b], ss4[:, b:b + 1], ffg, ALU.mult, ALU.mult)\
                       .then_inc(s_fin, 1)



_PARAMS = ("norm_mix_g", "gm_norm_g", "ml_conv_b", "ml_head_g", "ml_skip")


def _launch_arrays(i):
    import numpy as np

    a = {k: np.asarray(v) for k, v in i.items()}
    f = np.float32

    def by_feature(v):
        return v.reshape(L, NK, P).transpose(0, 2, 1)

    def by_tile(w):
        n = w.shape[2] // P
        return w.reshape(L, NK, P, n, P).transpose(0, 3, 2, 1, 4)

    par = np.zeros((L, P, NPAR), f)
    for n, name in enumerate(_PARAMS):
        par[:, :, 8 * n:8 * n + 8] = by_feature(a[name].reshape(L, D))
    cw = a["ml_conv_w"].reshape(L, CONV, NK, P).transpose(0, 3, 2, 1)
    par[:, :, P_CW:P_BG] = cw.reshape(L, P, NK * CONV)
    par[:, 0:NH, P_BG:] = a["ml_b_gate"].reshape(L, 4, NH).transpose(0, 2, 1)
    wg = np.zeros((L, D, P), f)
    for t in range(4):
        wg[:, :, 32 * t:32 * t + NH] = a["ml_w_gate"][:, :, NH * t:NH * (t + 1)]
    qkv = np.stack([a[n].reshape(L, NH, 2, P, DH) for n in ("ml_w_q", "ml_w_k", "ml_w_v")], axis=3)
    out = {
        "x_in": a["x"].reshape(S, D),
        "par": par,
        "bs": a["gm_b_s"],
        "ws": a["gm_w_s"].transpose(0, 3, 1, 2),
        "w_in": by_tile(a["w_in"]),
        "w_qkv": qkv.transpose(0, 1, 4, 3, 2, 5),
        "w_g": wg.reshape(L, NK, P, P).transpose(0, 2, 1, 3),
        "w_a": by_tile(a["w_branch_a"]),
        "w_b": by_tile(a["w_branch_b"]),
        "w_o": a["w_out"].reshape(L, 4, 2, P, 2, S).transpose(0, 4, 1, 3, 2, 5).reshape(L, 8, P, NK, P),
        "ffn_g": a["norm_ffn_g"],
        "w_pq": by_tile(a["peer_w_query"]),
        "keys": a["peer_sub_keys"].reshape(L, 2 * PH, KEYS, P).transpose(0, 3, 1, 2),
        "uv": np.concatenate([a["peer_u"], a["peer_v"]], axis=2).reshape(L * KEYS * KEYS, 2 * D),
        "fin_g": a["final_g"].reshape(1, D),
    }
    return {k: np.ascontiguousarray(v) for k, v in out.items()}


def kernel(**inputs):
    import concourse.bacc as bacc
    from concourse.bass_utils import run_bass_kernel_spmd as run

    nc = bacc.Bacc("TRN2", target_bir_lowering=False, num_devices=1)
    arrays = _launch_arrays(inputs)
    aps = {n: nc.dram_tensor(f"in_{n}", v.shape, mybir.dt.from_np(v.dtype), kind="ExternalInput").ap()
           for n, v in arrays.items()}
    out = nc.dram_tensor("out", (S, D), F32, kind="ExternalOutput").ap()
    build(nc, out=out, **aps)
    r = run(nc, [{f"in_{n}": v for n, v in arrays.items()}], core_ids=[0])
    return r.results[0]["out"].reshape(1, S, D)
```

```python
from contextlib import ExitStack

import concourse.bass as bass
from concourse import mybir

ALU = mybir.AluOpType
ACT = mybir.ActivationFunctionType
AX = mybir.AxisListType
F32 = mybir.dt.float32
F32R = mybir.dt.float32r
U32 = mybir.dt.uint32

P = 128
S = 512
D = 1024
NB = S // P
NK = D // P
L = 2
NH = 4
DH = D // NH
CONV = 5
PH = 8
KEYS = 128
TOPK = 16
EPS = 1e-6
LOWEST = -3.0e38
RAW, PARTS = 2, 3
SLOTS = 8
BATCH = 4
SIZE = 53200
NSEL = NB * PH

(P_MIXG, P_GMG, P_CB, P_HG, P_SK) = (8 * i for i in range(5))
P_FFG = 40
P_CW = 48
P_BG = P_CW + 8 * CONV
NPAR = P_BG + 4

QKV = ("q0", "q1", "k0", "k1", "v0", "v1")


def _each(*kinds, n=NK):
    return [(kind, j) for kind in kinds for j in range(n)]


FILLS = (_each("v", "xm", "u") + _each("vr", n=2 * NB) + _each("o", "mix", "ga", "gb")
         + [("gates", 0)] + [(n, 0) for n in QKV] + [("a", 0), ("a", 1), ("cols", 0)])
for _h in range(NH - 1):
    FILLS += [(n, _h + 1) for n in QKV] + [("a", 2 * _h + 2), ("a", 2 * _h + 3)]
FILLS += _each("b") + _each("pq", n=2 * PH)
AHEAD = 6 * NK + PARTS
SCORES_AT, EXPS_AT = (2, 4), (5, 9)
FILL_NO = {name: n for n, name in enumerate(FILLS)}

TILES = (_each("v", "xm", "u", "o", "ga", "gb") + _each("b", n=PARTS) + _each("a")
         + _each("b")[PARTS:] + _each("wo") + _each("pq", n=2 * PH))
SPLIT = [t for t in TILES if t[0] != "a"]
SPLIT_NO = {name: n for n, name in enumerate(SPLIT)}
TILE_NO = {name: n for n, name in enumerate(TILES)}
SECTION = {"u": 0, "v": 1, "xm": 2, "o": 3, "ga": 4, "gb": 5}


class Own:

    def __init__(self, eng):
        self.eng, self.n = eng, {}

    def tell(self, ins, sem):
        ins.then_inc(sem, 1)
        self.n[sem.name] = self.n.get(sem.name, 0) + 1

    def done(self, sem):
        self.eng.wait_ge(sem, self.n[sem.name])

    def link(self, ins, sem):
        self.tell(ins, sem)
        self.done(sem)

    def forget(self, sem):
        self.n[sem.name] = 0


def build(nc, x_in, par, bs, ws, w_in, w_qkv, w_g, w_a, w_b, w_o, ffn_g, w_pq, keys, uv, fin_g, out):
    ctx = ExitStack()
    with ctx:
        ctx.enter_context(nc.sbuf_tensor("reserved", [P, SIZE], F32))
        base = nc.sbuf_base - 4 * SIZE
        at = [0]

        def place(name, n, start, dtype=F32):
            return nc.alloc_sbuf_tensor_at(name, [P, n], dtype, offset=base + 4 * start)[:, :]

        def take(name, n):
            start, at[0] = at[0], at[0] + -(-n // 8) * 8
            return place(name, n, start)

        def rows(t):
            return t.rearrange("p (b d) -> p b d", b=NB)

        def chunks(t, n=NK):
            return t.rearrange("p (k t) -> p k t", k=n)

        X = rows(take("X", NB * D))
        at_R1 = at[0]
        R1 = take("R1", NK * S + 16)
        R2 = take("R2", NK * S)
        at_R3 = at[0]
        R3 = take("R3", NK * S)
        at_R4 = at[0]
        R4 = take("R4", NK * (S + 4))
        at_R5 = at[0]
        R5 = take("R5", NK * S)
        at_R6 = at[0]
        R6 = take("R6", NK * S)
        at_R7 = at[0]
        R7 = take("R7", NK * S)
        at_RW = at[0]
        RW = take("RW", (RAW + 2 * PARTS) * D)
        at_WQKV = at[0]
        WQKV = take("WQKV", 3 * 2 * DH).rearrange("p (m c e) -> p m c e", m=3, c=2)
        at_PW = at[0]
        PW = take("PW", 3 * D)
        HR = take("HR", NB * DH)
        at_G = at[0]
        G = [take(f"G{i}", 2 * S) for i in range(5)]
        sg = take("sg", S)
        sel = take("sel", NH * P).rearrange("p (h m) -> p h m", h=NH)
        ident = take("ident", P)
        prm = take("prm", NPAR)
        cols = take("cols", 64).rearrange("p (i d b h) -> p i d b h", i=2, d=2, b=NB)
        small = take("small", 64)
        unused = small[:, 48:49]
        eps = small[:, 61:62]
        row0 = small[:, 60:61]
        assert at[0] <= SIZE, at

        xcT = chunks(R7)
        h_rows, v_rows, gbT = rows(R2), rows(R2), chunks(R2)
        uT, oT = chunks(R3), chunks(R5)
        xmT = R4.rearrange("p (k t) -> p k t", k=NK)
        vT, gaT = chunks(R6), chunks(R6)
        raw = RW[:, 0:RAW * D].rearrange("p (r n) -> p r n", r=RAW)
        w_hi, w_lo = (place(name, PARTS * D, at_RW + (RAW + i * PARTS) * D, F32R)
                      .rearrange("p (r n) -> p r n", r=PARTS) for i, name in enumerate(("w_hi", "w_lo")))
        hT, ybT, mT, xnT = ([chunks(place(f"{name}_{part}", NK * S, start, F32R))
                             for part, start in zip(("hi", "lo"), starts)]
                            for name, starts in (("hT", (at_R1, at_G)), ("ybT", (at_R5, at_R7)),
                                                 ("mT", (at_R3, at_R4)), ("xnT", (at_R1, at_G))))
        wsT = PW[:, 0:D].rearrange("p (g t) -> p g t", g=NK)
        bsb = PW[:, D:2 * D].rearrange("p (g t) -> p g t", g=NK)
        wg = PW[:, 2 * D:3 * D].rearrange("p (k m) -> p k m", k=NK)
        qs, ks = (R1[:, i * 2 * S:(i + 1) * 2 * S].rearrange("p (c t) -> p c t", c=2) for i in range(2))
        VA = DH + 1
        vaug = [R1[:, 4 * S + i * NB * VA:4 * S + (i + 1) * NB * VA].rearrange("p (b e) -> p b e", b=NB)
                for i in range(2)]
        h_head = HR.rearrange("p (b e) -> p b e", b=NB)
        tmp = HR[:, 0:S]
        g_i, g_f, g_t, g_F, g_M = (g[0:NH].rearrange("p (d t) -> p d t", d=2) for g in G)
        junk = G[0]
        ffg = place("ffn_gain", D, at_WQKV)
        rdiag = sg.rearrange("p (b m) -> p b m", b=NB)
        work = place("work", NK * S, at_PW)
        ss1, ss2, ss3, ss4 = (small[:, 4 * i:4 * i + 4] for i in range(4))
        den = small[:, 16:24]
        hss, ss5 = small[:, 24:28], small[:, 28:32]
        iota16 = small[:, 32:48]

        def attn(d, c):
            n = (NB - c) * P if d == 0 else (c + 1) * P
            off = sum((NB - i) * P for i in range(c)) if d == 0 else 10 * P + sum((i + 1) * P for i in range(c))
            return PW[:, off:off + n], (c * P if d == 0 else 0), n

        xn = rows(R2)
        q_flat = place("queries", 2 * PH * S, at_R3)
        qT = q_flat.rearrange("p (b m t) -> p b m t", b=NB, m=2 * PH)
        q_heads = q_flat.rearrange("p (n c) -> p n c", n=NSEL)
        slot = place("slots", SLOTS * 2 * D, at_R6).rearrange("p (r w d) -> p r w d", r=SLOTS, w=2)
        keysT = R5[:, 0:2 * PH * KEYS].rearrange("p (m k) -> p m k", m=2 * PH)
        q_now = R5[:, 2048:2560].rearrange("p (y h t) -> p y h t", y=2, h=2)
        x_now = R5[:, 2560:3584]
        diag = work[:, 0:2 * BATCH * P].rearrange("p (y s m) -> p y s m", y=2, s=BATCH)
        o_ = [2 * BATCH * P]

        def piece(n):
            o_[0] += n
            return work[:, o_[0] - n:o_[0]]
        sc2 = piece(256).rearrange("p (h k) -> p h k", h=2)
        sc2r = piece(KEYS)
        cand, cand2 = piece(256), piece(256)
        onehot, picked = (piece(512).rearrange("p (h k j) -> p h k j", h=2, k=TOPK) for _ in range(2))
        sv = piece(32).rearrange("p (h k) -> p h k", h=2)
        si = piece(32).bitcast(U32).rearrange("p (h k) -> p h k", h=2)
        cv = piece(16)
        ci = piece(16).bitcast(U32)
        cab = piece(32).bitcast(U32).rearrange("p (h k) -> p h k", h=2)
        pick = piece(32).rearrange("p (h k) -> p h k", h=2)
        idx = piece(32).bitcast(U32).rearrange("p (y k) -> p y k", y=2)
        ex = piece(16)
        gate = piece(32).rearrange("p (y k) -> p y k", y=2)
        esum, ncv, rin = piece(1), piece(1), piece(1)
        dots = piece(32).rearrange("p (y k) -> p y k", y=2)
        acts = piece(32).rearrange("p (y k) -> p y k", y=2)
        wt = piece(32).rearrange("p (y k) -> p y k", y=2)
        assert o_[0] <= NK * S

        ps = [ctx.enter_context(nc.psum_tensor(f"bank{i}", [P, S], F32))[:, :] for i in range(8)]
        bank = ps[0:2]
        ps_s = ps[2:4]
        ps_a = ps[4:6]
        ps_n = ps[6:8]
        ps_v = ps[0:2]
        ps_k = ps[2:4]

        def sem(name):
            return ctx.enter_context(nc.semaphore(name))

        s_x, s_out, s_pool = sem("x_loaded"), sem("out_stored"), sem("pool_constants")
        filled = [sem(f"bank_filled{i}") for i in range(2)]
        drained = [sem(f"bank_drained{i}") for i in range(2)]
        s_par, s_ffg, s_keys = sem("params_loaded"), sem("ffn_gain_loaded"), sem("keys_loaded")
        s_w = [sem(f"weights_loaded{i}") for i in range(RAW)]
        s_whi, s_wlo = sem("weights_hi"), sem("weights_lo")
        s_hhi, s_ybhi, s_mval, s_mhi, s_xhi = sem("h_hi"), sem("yb_hi"), sem("merged"), sem("merged_hi"), sem("x_hi")
        s_ybval = sem("yb_value")
        s_tfull, s_tlow = sem("turned"), sem("turned_lo")
        s_hdfull, s_hdout = sem("head_turned"), sem("head_taken")
        s_sg = sem("conv_sigmoid")
        s_wotile, s_wosum, s_wofree = sem("wo_tile_used"), sem("wo_summed"), sem("wo_added")
        s_qkvw = sem("qkv_weights_loaded")
        s_a, s_d = sem("act_step"), sem("dve_step")
        s_sq, s_sqd, s_sqv, s_sqx = (sem(n) for n in ("h_squares", "h_squares_dve", "v_squares", "x_squares"))
        s_rdiag, s_vs, s_xr = sem("rstd_diagonal"), sem("v_rows_scaled"), sem("x_rows_ready")
        s_sqsum = sem("x_squares_summed")
        s_ya, s_yb = sem("ya_ready"), sem("yb_ready")
        s_conv, s_xc = sem("conv_done"), sem("xc_ready")
        s_gin, s_nabs, s_ln = sem("gates_in"), sem("gates_negabs"), sem("gates_ln")
        s_fm, s_rows = sem("gates_stabiliser"), sem("gates_rows_ready")
        s_em = sem("gates_em_ready")
        s_afull, s_afree = sem("a_full"), sem("a_free")
        s_arg, s_exp, s_mask, s_p = sem("attn_arg"), sem("attn_exp"), sem("attn_masked"), sem("attn_ready")
        s_sfull = sem("scores_full")
        s_nfull, s_nfree = sem("num_full"), sem("num_free")
        s_hsum, s_hsq, s_hn = sem("head_summed"), sem("head_squares"), sem("head_normed")
        s_xs = sem("xc_skip")
        s_one = sem("vaug_ones")
        s_table, s_std, s_rstd = sem("sqrt_table"), sem("std_ready"), sem("rstd_ready")
        s_clear_last = sem("layer_end")
        s_gather = [sem(f"gathered{i}") for i in range(SLOTS)]
        s_free = sem("slots_free")
        s_idx = sem("indices_ready")
        s_dot, s_act, s_diag = sem("dots_ready"), sem("gelu_ready"), sem("diag_ready")
        s_q, s_sc = sem("query_staged"), sem("key_scores_ready")
        s_cv, s_ex = sem("top_ready"), sem("exp_ready")
        s_vfree = sem("block_added")
        s_ps = sem("peer_dve_step")
        s_vfree0 = sem("row0_set")
        s_fsq, s_fin = sem("final_squares"), sem("final_ready")
        s_fstd, s_frs = sem("final_std"), sem("final_rstd")
        first, last_ = filled[0], s_clear_last

        def is_filled(eng, *name):
            n = FILL_NO[name]
            eng.wait_ge(filled[n % 2], n // 2 + 1)
            return bank[n % 2]

        def drain(ins, *name):
            ins.then_inc(drained[FILL_NO[name] % 2], 1)

        def is_drained(eng, *name):
            n = FILL_NO[name]
            eng.wait_ge(drained[n % 2], n // 2 + 1)

        def loaded(eng, name):
            n = TILE_NO[name]
            eng.wait_ge(s_w[n % RAW], 16 * (n // RAW + 1))
            return raw[:, n % RAW]

        def is_multiplied(eng, m):
            kind, j = SPLIT[m]
            if kind == "wo":
                half, m4 = j // 4, j % 4
                if m4 == 3:
                    eng.wait_ge(s_wosum, NB * (half + 1))
                else:
                    eng.wait_ge(s_wotile, 3 * half + m4 + 1)
            else:
                is_filled(eng, kind, j)

        with nc.Block() as block:
            @block.sync
            def _(sp):
                sp.dma_start(X, x_in.rearrange("(b p) d -> p b d", p=P)).then_inc(s_x, 16)

            @block.gpsimd
            def _(pool):
                pool.memset(ident, 0.0).then_inc(s_pool, 1)
                pool.memset(sel, 1.0).then_inc(s_pool, 1)
                pool.wait_ge(s_pool, 2)
                pool.affine_select(out=ident, in_=ident, compare_op=ALU.not_equal, fill=1.0, base=0,
                                   pattern=[[-1, P]], channel_multiplier=1).then_inc(s_pool, 1)
                pool.affine_select(out=sel, in_=sel, compare_op=ALU.is_equal, fill=0.0, base=0,
                                   pattern=[[-1, NH], [0, P]], channel_multiplier=1).then_inc(s_pool, 1)
                pool.iota(iota16, [[1, TOPK]], base=0, channel_multiplier=0,
                          allow_small_or_imprecise_dtypes=True).then_inc(s_pool, 1)
                pool.wait_ge(s_pool, 5)

            @block.tensor
            def _(pe):
                pe.sem_inc(s_vfree, 2)

            @block.vector
            def _(dve):
                dve.memset(row0, 0.0).then_inc(s_vfree0, 1)
                dve.memset(eps, EPS).then_inc(s_vfree0, 1)
                dve.wait_ge(s_vfree0, 2)
                dve.wait_ge(s_x, 16)

        with nc.Fori(0, L) as l:
            def numbers(b, hp, y):
                n = b * PH + hp * 2 + y
                return n, l * NSEL + n

            with nc.Block() as block:
                @block.sync
                def _(sp):
                    lay = bass.ds(l, 1)
                    sp.dma_start(prm, par[lay].rearrange("l p c -> (l p) c")).then_inc(s_par, 16)
                    sp.dma_start(wsT, ws[lay].rearrange("l p g t -> (l p) g t")).then_inc(s_par, 16)
                    sp.dma_start(bsb, bs[lay].rearrange("l g t -> l (g t)").to_broadcast([P, D])
                                 .rearrange("p (g t) -> p g t", g=NK)).then_inc(s_par, 16)
                    sp.dma_start(wg, w_g[lay].rearrange("l p k m -> (l p) k m")).then_inc(s_par, 16)

                    def load_qkv(h):
                        if h >= 1:
                            is_filled(sp, "v1", h - 1)
                        sp.dma_start(WQKV, w_qkv[lay, h].rearrange("l p m c e -> (l p) m c e"))\
                          .then_inc(s_qkvw, 16)

                    for n, (kind, j) in enumerate(TILES):
                        if kind == "ga" and j == 0:
                            load_qkv(0)
                        if kind == "a" and j >= 2 and j % 2 == 0:
                            load_qkv(j // 2)
                        if n >= RAW:
                            old = TILES[n - RAW]
                            if old[0] == "a":
                                is_filled(sp, *old)
                            else:
                                sp.wait_ge(s_wlo, SPLIT_NO[old] + 1)
                        if kind == "pq" and j == 0:
                            is_filled(sp, "b", NK - 1)
                            sp.dma_start(keysT, keys[lay].rearrange("l p m k -> (l p) m k")).then_inc(s_keys, 16)
                        if kind in SECTION:
                            src = w_in[lay, SECTION[kind] * NK + j]
                        elif kind == "wo":
                            src = w_o[lay, j]
                        else:
                            src = {"a": w_a, "b": w_b, "pq": w_pq}[kind][lay, j]
                        sp.dma_start(raw[:, n % RAW], src.rearrange("l p k c -> (l p) (k c)"))\
                          .then_inc(s_w[n % RAW], 16)
                        if kind == "a" and j == NK - 1:
                            is_filled(sp, "v1", NH - 1)
                            sp.dma_start(ffg, ffn_g[lay].to_broadcast([P, D])).then_inc(s_ffg, 16)
                    sp.wait_ge(s_keys, 16)

                @block.gpsimd
                def _(pool):
                    def lows(kinds):
                        for m, name in enumerate(SPLIT):
                            if name in kinds:
                                pool.wait_ge(s_whi, m + 1)
                                w = loaded(pool, name)
                                pool.tensor_tensor(w_lo[:, m % PARTS], w, w_hi[:, m % PARTS].bitcast(F32),
                                                   ALU.subtract).then_inc(s_wlo, 1)

                    pool.memset(xmT[:, :, 0:2], 0.0).then_inc(s_one, 1)
                    pool.memset(xmT[:, :, S + 2:S + 4], 0.0).then_inc(s_one, 1)
                    lows(SPLIT[:AHEAD])
                    is_filled(pool, "gb", NK - 1)
                    for i in range(2):
                        pool.memset(vaug[i][:, :, DH:VA], 1.0).then_inc(s_one, 1)
                    for h in range(NH):
                        for c in range(NB):
                            for d in range(2):
                                w, t0, n = attn(d, c)
                                o = 0 if d == 0 else c * P
                                sgn = 1 if d == 0 else -1
                                pool.wait_ge(s_exp, 8 * h + 2 * c + d + 1)
                                pool.affine_select(out=w[:, o:o + P], in_=w[:, o:o + P], compare_op=ALU.is_ge,
                                                   fill=0.0, base=0, pattern=[[sgn, P]],
                                                   channel_multiplier=-sgn).then_inc(s_mask, 1)
                    lows(SPLIT[AHEAD:])

                    want_free, want_idx = pool.alloc_register("want_free"), pool.alloc_register("want_idx")
                    pool.reg_mov(want_free, l * (NSEL * TOPK + SLOTS) + 1)
                    pool.reg_mov(want_idx, l * (NSEL + 1) + 1)
                    with pool.Fori(0, NSEL // 2) as pair:
                        for y in range(2):
                            pool.wait_ge(s_idx, want_idx)
                            pool.reg_add(want_idx, want_idx, 1)
                            for k in range(TOPK):
                                pool.wait_ge(s_free, want_free)
                                pool.reg_add(want_free, want_free, 1)
                                pool.indirect_dma_start(
                                    out=slot[:, k % SLOTS].rearrange("p w d -> p (w d)"), out_offset=None, in_=uv,
                                    in_offset=bass.IndirectOffsetOnAxis(ap=idx[:, y, k:k + 1], axis=0))\
                                    .then_inc(s_gather[k % SLOTS], 16)

                @block.scalar
                def _(act):
                    own = Own(act)

                    def std(ss, n):
                        act.activation(ss, ss, ACT.Sqrt, bias=eps, scale=1.0 / n).then_inc(s_std, 1)

                    def load_sqrt():
                        own.link(act.activation(unused, eps, ACT.Sqrt), s_table)

                    def prepare(m):
                        if m >= len(SPLIT):
                            return
                        w = loaded(act, SPLIT[m])
                        if m >= PARTS:
                            is_multiplied(act, m - PARTS)
                        act.activation(w_hi[:, m % PARTS], w, ACT.Copy).then_inc(s_whi, 1)

                    def section(kind, out, func):
                        for j in range(NK):
                            if SPLIT_NO[(kind, j)] + 2 < AHEAD:
                                prepare(SPLIT_NO[(kind, j)] + 2)
                            drain(act.activation(out(j), is_filled(act, kind, j), func), kind, j)

                    for b in range(NB // 2):
                        act.activation(h_rows[:, b], X[:, b], ACT.Square, accum_out=ss1[:, b:b + 1])\
                           .then_inc(s_sq, 1)
                    act.wait_ge(s_sq, NB // 2)
                    act.wait_ge(s_sqd, NB // 2)
                    std(ss1, D)
                    prepare(0)
                    prepare(1)
                    act.wait_ge(s_par, 64)
                    for k in range(NK):
                        act.wait_ge(s_tfull, k + 1)
                        act.activation(hT[0][:, k], ps[k], ACT.Copy,
                                       scale=prm[:, P_MIXG + k:P_MIXG + k + 1]).then_inc(s_hhi, 1)
                    section("v", lambda j: vT[:, j], ACT.Gelu_apprx_tanh)
                    section("xm", lambda j: xmT[:, j, 2:S + 2], ACT.Copy)
                    section("u", lambda j: uT[:, j], ACT.Gelu_apprx_tanh)
                    for b in range(NB):
                        drain(act.activation(v_rows[:, b, S:D], is_filled(act, "vr", 2 * b + 1), ACT.Copy),
                              "vr", 2 * b + 1)
                        is_drained(act, "vr", 2 * b)
                        is_drained(act, "vr", 2 * b + 1)
                        if b:
                            act.wait_ge(s_sqv, b)
                        act.activation(HR, v_rows[:, b], ACT.Square, accum_out=ss2[:, b:b + 1])\
                           .then_inc(s_sqv, 1)
                    act.wait_ge(s_sqv, NB)
                    std(ss2, D)
                    def conv_sigmoid(j):
                        act.wait_ge(s_conv, j + 1)
                        if j:
                            act.wait_ge(s_xc, j)
                        act.activation(sg, xcT[:, j], ACT.Sigmoid).then_inc(s_sg, 1)

                    section("o", lambda j: oT[:, j], ACT.Sigmoid)
                    section("ga", lambda j: gaT[:, j], ACT.Sigmoid)
                    for j in range(NK):
                        conv_sigmoid(j)
                        prepare(SPLIT_NO[("gb", j)] + 2)
                        drain(act.activation(gbT[:, j], is_filled(act, "gb", j), ACT.Sigmoid), "gb", j)
                    prepare(AHEAD - 1)
                    z = is_filled(act, "gates", 0)
                    for i, (g, d) in enumerate(((g_i, 0), (g_f, 0), (g_i, 1), (g_f, 1))):
                        ins = act.activation(g[:, d], z[32 * i:32 * i + NH, :], ACT.Identity,
                                             bias=prm[0:NH, P_BG + i:P_BG + i + 1])
                        if i < 3:
                            ins.then_inc(s_gin, 1)
                        else:
                            drain(ins, "gates", 0)
                    act.wait_ge(s_nabs, 1)
                    act.activation(g_t, g_t, ACT.Exp).then_inc(s_a, 1)
                    act.wait_ge(s_a, 1)
                    act.activation(g_t, g_t, ACT.Ln, bias=1.0).then_inc(s_ln, 1)
                    def evacuate_qkv(h):
                        for e in range(2):
                            drain(act.activation(qs[:, e], is_filled(act, f"q{e}", h)[:, :], ACT.Copy), f"q{e}", h)
                        for e in range(2):
                            drain(act.activation(ks[:, e], is_filled(act, f"k{e}", h)[:, :], ACT.Copy,
                                                 scale=float(DH) ** -0.5), f"k{e}", h)
                        for i in range(2):
                            z = is_filled(act, f"v{i}", h)
                            drain(act.activation(vaug[h % 2][:, 2 * i:2 * i + 2, 0:DH],
                                                 z.rearrange("p (b e) -> p b e", b=2), ACT.Copy), f"v{i}", h)
                    evacuate_qkv(0)
                    act.wait_ge(s_fm, 1)
                    act.activation(g_t, g_t, ACT.Exp, scale=-1.0).then_inc(s_em, 1)
                    for h in range(NH):
                        for c in range(NB):
                            for d in range(2):
                                w, t0, n = attn(d, c)
                                act.wait_ge(s_arg, 8 * h + 2 * c + d + 1)
                                act.activation(w, w, ACT.Exp).then_inc(s_exp, 1)
                        if h + 1 < NH:
                            evacuate_qkv(h + 1)
                        for e in range(2):
                            f = 2 * h + e
                            act.activation(xcT[:, f], xcT[:, f], ACT.Copy,
                                           scale=prm[:, P_SK + f:P_SK + f + 1]).then_inc(s_xs, 1)
                        act.wait_ge(s_hsum, NB * (h + 1))
                        for b in range(NB):
                            if h or b:
                                act.wait_ge(s_hsq, NB * h + b)
                            act.activation(junk[:, 0:DH], h_head[:, b], ACT.Square,
                                           accum_out=hss[:, b:b + 1]).then_inc(s_hsq, 1)
                        act.wait_ge(s_hsq, NB * (h + 1))
                        std(hss, DH)

                    def hi(out, value, ready, n, sem_):
                        act.wait_ge(ready, n)
                        act.activation(out, value, ACT.Copy).then_inc(sem_, 1)

                    for j in range(NK):
                        prepare(SPLIT_NO[("b", j)] + PARTS)
                        if j:
                            hi(mT[0][:, j - 1], gaT[:, j - 1], s_mval, j, s_mhi)
                    hi(mT[0][:, NK - 1], gaT[:, NK - 1], s_mval, NK, s_mhi)

                    def squares(half):
                        for b in range(NB):
                            i = half * NB + b
                            act.wait_ge(s_wofree, i + 1)
                            act.activation(work[:, i * S:(i + 1) * S], X[:, b, half * S:(half + 1) * S], ACT.Square,
                                           accum_out=(ss3, ss5)[half][:, b:b + 1]).then_inc(s_sqx, 1)

                    for j in range(NK):
                        if j == NK // 2 + 1:
                            squares(0)
                            load_sqrt()
                        if j == NK - 1:
                            squares(1)
                        prepare(SPLIT_NO[("wo", j)] + PARTS)
                    act.wait_ge(s_sqsum, 1)
                    std(ss3, D)
                    for k in range(NK):
                        act.wait_ge(s_tfull, NK + k + 1)
                        act.activation(xnT[0][:, k], ps[k], ACT.Copy,
                                       scale=prm[:, P_FFG + k:P_FFG + k + 1]).then_inc(s_xhi, 1)

                    def stage(m, y, before):
                        if before is not None:
                            act.wait_ge(s_sc, before)
                        act.activation(q_now[:, y].rearrange("p h t -> p (h t)"), q_heads[:, m], ACT.Copy)\
                           .then_inc(s_q, 1)

                    def exps(count):
                        act.wait_ge(s_cv, count)
                        act.activation(ex, cv, ACT.Exp, bias=ncv, accum_out=esum).then_inc(s_ex, 1)

                    sel0 = l * (NSEL + 2)
                    for j in range(2 * PH):
                        prepare(SPLIT_NO[("pq", j)] + PARTS)
                        z = is_filled(act, "pq", j)
                        drain(act.activation(qT[:, :, j], z.rearrange("p (b t) -> p b t", b=NB), ACT.Copy), "pq", j)
                        if j in (1, 3):
                            is_drained(act, "pq", j - 1)
                            is_drained(act, "pq", j)
                            stage(j // 2, j // 2, None)
                        if j in EXPS_AT:
                            exps(sel0 + EXPS_AT.index(j) + 1)
                    is_drained(act, "pq", 2 * PH - 2)
                    is_drained(act, "pq", 2 * PH - 1)
                    with act.Fori(0, NB) as b:
                        with act.Fori(0, PH // 2) as hp:
                            for y in range(2):
                                n, N = numbers(b, hp, y)
                                stage((n + 2) % NSEL, y, sel0 + n + 1)
                                for q in range(4):
                                    act.wait_ge(s_dot, N * 4 + q + 1)
                                    act.activation(acts[:, y, 4 * q:4 * q + 4], dots[:, y, 4 * q:4 * q + 4],
                                                   ACT.Gelu_apprx_tanh).then_inc(s_act, 1)
                                exps(sel0 + n + 3)
                        act.wait_ge(s_free, l * SLOTS + (l * NB + b) * (PH * TOPK) + PH * TOPK + SLOTS)
                        for half in range(2):
                            act.activation(X[:, b, half * S:(half + 1) * S], ps_v[half], ACT.Copy).then_inc(s_vfree, 1)
                    load_sqrt()

                @block.vector
                def _(dve):
                    own = Own(dve)

                    def rstd(ss, n):
                        dve.wait_ge(s_std, n)
                        own.link(dve.reciprocal(ss, ss), s_rstd)

                    def rstd_diagonal(ss, n):
                        rstd(ss, n)
                        dve.tensor_tensor(rdiag, ident.unsqueeze(1).to_broadcast([P, NB, P]),
                                          ss.unsqueeze(2).to_broadcast([P, NB, P]), ALU.mult).then_inc(s_rdiag, 1)

                    def lows(pair, gain, s_hi):
                        for k in range(NK):
                            dve.wait_ge(s_hi, k + 1)
                            dve.scalar_tensor_tensor(pair[1][:, k], ps[k], prm[:, gain + k:gain + k + 1],
                                                     pair[0][:, k].bitcast(F32), ALU.mult, ALU.subtract)\
                               .then_inc(s_tlow, 1)

                    for b in range(NB // 2, NB):
                        dve.tensor_tensor_reduce(h_rows[:, b], X[:, b], X[:, b], 1.0, 0.0, ALU.mult, ALU.add,
                                                 ss1[:, b:b + 1]).then_inc(s_sqd, 1)
                    rstd_diagonal(ss1, 1)
                    dve.wait_ge(s_par, 64)
                    lows(hT, P_MIXG, s_hhi)
                    dve.wait_ge(s_one, 2)
                    for j in range(NK):
                        is_drained(dve, "xm", j)
                        cw = prm[:, P_CW + CONV * j:P_CW + CONV * (j + 1)]
                        own.link(dve.tensor_scalar(xcT[:, j], xmT[:, j, 0:S], cw[:, 0:1],
                                                   prm[:, P_CB + j:P_CB + j + 1], ALU.mult, ALU.add), s_d)
                        for w in range(1, CONV):
                            ins = dve.scalar_tensor_tensor(xcT[:, j], xmT[:, j, w:w + S], cw[:, w:w + 1],
                                                           xcT[:, j], ALU.mult, ALU.add)
                            if w < CONV - 1:
                                own.link(ins, s_d)
                            else:
                                ins.then_inc(s_conv, 1)
                    for b in range(NB):
                        drain(dve.tensor_copy(v_rows[:, b, 0:S], is_filled(dve, "vr", 2 * b)), "vr", 2 * b)
                    rstd(ss2, 2)
                    for b in range(NB):
                        dve.tensor_scalar(v_rows[:, b], v_rows[:, b], ss2[:, b:b + 1], None, ALU.mult)\
                           .then_inc(s_vs, 1)
                    for g in range(NK):
                        z = is_filled(dve, "mix", g)
                        if g:
                            dve.wait_ge(s_ya, g)
                        t3 = tmp.rearrange("p (b t) -> p b t", b=NB)
                        drain(dve.scalar_tensor_tensor(t3, z.rearrange("p (b t) -> p b t", b=NB),
                                                       prm[:, P_GMG + g:P_GMG + g + 1],
                                                       bsb[:, g].unsqueeze(1).to_broadcast([P, NB, P]),
                                                       ALU.mult, ALU.add), "mix", g)
                        is_drained(dve, "mix", g)
                        is_drained(dve, "u", g)
                        dve.tensor_tensor(uT[:, g], tmp, uT[:, g], ALU.mult).then_inc(s_ya, 1)
                    for j in range(NK):
                        dve.wait_ge(s_sg, j + 1)
                        dve.tensor_tensor(xcT[:, j], xcT[:, j], sg, ALU.mult).then_inc(s_xc, 1)
                    is_drained(dve, "gates", 0)
                    dve.wait_ge(s_gin, 3)
                    dve.scalar_tensor_tensor(g_t, g_f, -1.0, g_f, ALU.mult, ALU.min).then_inc(s_nabs, 1)
                    dve.wait_ge(s_ln, 1)
                    own.link(dve.scalar_tensor_tensor(g_f, g_f, 0.0, g_t, ALU.min, ALU.subtract), s_d)
                    way = (slice(None), slice(None, None, -1))
                    for d in range(2):
                        own.link(dve.tensor_tensor_scan(g_F[:, d, way[d]], g_f[:, d, way[d]], g_f[:, d, way[d]],
                                                        0.0, ALU.add, ALU.bypass), s_d)
                    own.link(dve.tensor_tensor(g_i, g_i, g_F, ALU.subtract), s_d)
                    for d in range(2):
                        own.link(dve.tensor_tensor_scan(g_M[:, d, way[d]], g_i[:, d, way[d]], g_i[:, d, way[d]],
                                                        0.0, ALU.max, ALU.max), s_d)
                    dve.tensor_tensor(g_t, g_F, g_M, ALU.add).then_inc(s_fm, 1)
                    dve.tensor_scalar(g_f, g_M, -1.0, None, ALU.mult).then_inc(s_rows, 1)

                    def branch_a(j):
                        drain(dve.tensor_tensor(gaT[:, j], is_filled(dve, "a", j), gaT[:, j], ALU.mult), "a", j)

                    def head_out(f):
                        dve.wait_ge(s_hdfull, f + 1)
                        dve.wait_ge(s_xs, f + 1)
                        own.link(dve.scalar_tensor_tensor(xcT[:, f], ps_a[f % 2], prm[:, P_HG + f:P_HG + f + 1],
                                                          xcT[:, f], ALU.mult, ALU.add), s_hdout)
                        own.link(dve.tensor_tensor(xcT[:, f], oT[:, f], xcT[:, f], ALU.mult), s_ybval)
                        own.link(dve.tensor_copy(ybT[0][:, f], xcT[:, f]), s_ybhi)
                        dve.tensor_tensor(ybT[1][:, f], xcT[:, f], ybT[0][:, f].bitcast(F32), ALU.subtract)\
                           .then_inc(s_yb, 1)

                    branch_a(0)
                    branch_a(1)
                    z = is_filled(dve, "cols", 0)
                    drain(dve.tensor_copy(cols.rearrange("p i d b h -> p (i d b h)"), z[:, 0:64]), "cols", 0)
                    is_drained(dve, "cols", 0)

                    def arguments(h):
                        dve.wait_ge(s_afull, h + 1)
                        for c in range(NB):
                            for d in range(2):
                                w, t0, n = attn(d, c)
                                dve.tensor_scalar(w, ps_a[d][:, t0:t0 + n], cols[:, 0, d, c, h:h + 1], 0.0,
                                                  ALU.add, ALU.min).then_inc(s_arg, 1)

                    arguments(0)
                    for h in range(NH):
                        if h:
                            branch_a(2 * h)
                            branch_a(2 * h + 1)
                        for c in range(NB):
                            dve.wait_ge(s_sfull, NB * h + c + 1)
                            for d in range(2):
                                w, t0, n = attn(d, c)
                                dve.wait_ge(s_mask, 8 * h + 2 * c + d + 1)
                                dve.tensor_tensor(w, w, ps_s[c % 2][:, t0:t0 + n], ALU.mult).then_inc(s_p, 1)
                        if h:
                            head_out(2 * h - 2)
                            head_out(2 * h - 1)
                        for i in range(2 * NB):
                            d, b = i // NB, i % NB
                            dve.wait_ge(s_nfull, 8 * h + i + 1)
                            n_ = ps_n[i % 2]
                            own.link(dve.tensor_scalar(den[:, i:i + 1], n_[:, DH:VA], -1.0,
                                                       cols[:, 1, d, b, h:h + 1], ALU.mult, ALU.max), s_d)
                            own.link(dve.tensor_tensor(den[:, i:i + 1], den[:, i:i + 1], n_[:, DH:VA], ALU.max), s_d)
                            own.link(dve.reciprocal(den[:, i:i + 1], den[:, i:i + 1]), s_d)
                            if d == 0:
                                own.link(dve.tensor_scalar(h_head[:, b], n_[:, 0:DH], den[:, i:i + 1], None,
                                                           ALU.mult), s_nfree)
                            else:
                                dve.wait_ge(s_nfree, 4 * h + 4)
                                own.link(dve.scalar_tensor_tensor(h_head[:, b], n_[:, 0:DH], den[:, i:i + 1],
                                                                  h_head[:, b], ALU.mult, ALU.add), s_hsum)
                        if h + 1 < NH:
                            arguments(h + 1)
                        rstd(hss, 3 + h)
                        dve.tensor_tensor(h_head, h_head, hss.unsqueeze(2).to_broadcast([P, NB, DH]),
                                          ALU.mult).then_inc(s_hn, 1)
                    head_out(2 * NH - 2)
                    head_out(2 * NH - 1)

                    def merged_lo(j):
                        dve.wait_ge(s_mhi, j + 1)
                        dve.tensor_tensor(mT[1][:, j], gaT[:, j], mT[0][:, j].bitcast(F32), ALU.subtract)\
                           .then_inc(s_ya, 1)

                    for j in range(NK):
                        drain(dve.tensor_tensor(gbT[:, j], is_filled(dve, "b", j), gbT[:, j], ALU.mult), "b", j)
                        is_drained(dve, "b", j)
                        own.link(dve.tensor_tensor(gaT[:, j], gaT[:, j], gbT[:, j], ALU.add), s_mval)
                        if j:
                            merged_lo(j - 1)
                    merged_lo(NK - 1)
                    for i in range(2 * NB):
                        half, b = i // NB, i % NB
                        xs = X[:, b, half * S:(half + 1) * S]
                        dve.wait_ge(s_wosum, i + 1)
                        dve.tensor_tensor(xs, xs, ps[4 + b], ALU.add).then_inc(s_wofree, 1)
                    dve.wait_ge(s_sqx, 2 * NB)
                    dve.tensor_tensor(ss3, ss3, ss5, ALU.add).then_inc(s_sqsum, 1)
                    rstd_diagonal(ss3, 3 + NH)
                    lows(xnT, P_FFG, s_xhi)
                    dve.wait_ge(s_ffg, 16)
                    for b in range(NB):
                        dve.scalar_tensor_tensor(xn[:, b], X[:, b], ss3[:, b:b + 1], ffg, ALU.mult, ALU.mult)\
                           .then_inc(s_xr, 1)

                    def step(ins):
                        own.link(ins, s_ps)

                    def top16(values, rest, best, where):
                        step(dve.max(best[:, 0:8], values))
                        step(dve.max_index(where[:, 0:8], best[:, 0:8], values))
                        step(dve.match_replace(rest, best[:, 0:8], values, LOWEST))
                        step(dve.max(best[:, 8:16], rest))
                        step(dve.max_index(where[:, 8:16], best[:, 8:16], rest))

                    def choose_first(y, scored):
                        dve.wait_ge(s_sc, scored)
                        step(dve.tensor_copy(sc2.rearrange("p h k -> p (h k)"), ps_k[y][:, 0:2 * KEYS]))
                        top16(sc2[:, 0], sc2r, sv[:, 0], si[:, 0])

                    def choose_second():
                        top16(sc2[:, 1], sc2r, sv[:, 1], si[:, 1])
                        step(dve.tensor_tensor(cand.rearrange("p (i j) -> p i j", i=TOPK),
                                               sv[:, 0].unsqueeze(2).to_broadcast([P, TOPK, TOPK]),
                                               sv[:, 1].unsqueeze(1).to_broadcast([P, TOPK, TOPK]), ALU.add))

                    def choose_pairs():
                        top16(cand, cand2, cv, ci)
                        dve.tensor_scalar(ncv, cv[:, 0:1], -1.0, None, ALU.mult).then_inc(s_cv, 1)

                    def find_rows(y):
                        step(dve.tensor_scalar(cab[:, 0], ci, 4, None, ALU.logical_shift_right))
                        step(dve.tensor_scalar(cab[:, 1], ci, TOPK - 1, None, ALU.bitwise_and))
                        full4 = [P, 2, TOPK, TOPK]
                        for h in range(2):
                            step(dve.tensor_tensor(onehot[:, h], iota16.unsqueeze(1).to_broadcast(full4[:1] + full4[2:]),
                                                   cab[:, h].unsqueeze(2).to_broadcast(full4[:1] + full4[2:]),
                                                   ALU.is_equal))
                        step(dve.tensor_tensor(picked, onehot, si.unsqueeze(2).to_broadcast(full4), ALU.mult))
                        step(dve.tensor_reduce(pick.rearrange("p h k -> p (h k)"),
                                               picked.rearrange("p h k j -> p (h k) j"), AX.X, ALU.add))
                        step(dve.tensor_scalar(pick[:, 0], pick[:, 0], float(KEYS), row0, ALU.mult, ALU.add))
                        dve.tensor_tensor(idx[:, y], pick[:, 0], pick[:, 1], ALU.add).then_inc(s_idx, 1)

                    def set_gate(y, exped):
                        dve.wait_ge(s_ex, exped)
                        step(dve.tensor_copy(rin, esum))
                        step(dve.reciprocal(rin, rin))
                        step(dve.tensor_scalar(gate[:, y], ex, rin, None, ALU.mult))

                    def next_round():
                        own.done(s_ps)
                        dve.sem_clear(s_ps)
                        own.forget(s_ps)

                    sel0 = l * (NSEL + 2)
                    choose_first(0, sel0 + 1)
                    choose_second()
                    choose_pairs()
                    find_rows(0)
                    set_gate(0, sel0 + 1)
                    choose_first(1, sel0 + 2)
                    choose_second()
                    choose_pairs()
                    next_round()
                    dve.wait_ge(s_xr, NB)
                    with dve.Fori(0, NB) as b:
                        step(dve.tensor_copy(x_now, xn[:, b]))
                        next_round()
                        with dve.Fori(0, PH // 2) as hp:
                            for y in range(2):
                                n, N = numbers(b, hp, y)
                                for q in range(4):
                                    for k in range(4):
                                        r = (4 * q + k) % SLOTS
                                        dve.wait_ge(s_gather[r], N * 32 + 16 * (q // 2) + 16)
                                        ins = dve.tensor_tensor_reduce(slot[:, r, 0], slot[:, r, 0], x_now, 1.0, 0.0,
                                                                       ALU.mult, ALU.add,
                                                                       dots[:, y, 4 * q + k:4 * q + k + 1])
                                    ins.then_inc(s_dot, 1)
                                    dve.wait_ge(s_act, N * 4 + q + 1)
                                    sl = slice(4 * q, 4 * q + 4)
                                    step(dve.tensor_tensor(wt[:, y, sl], acts[:, y, sl], gate[:, y, sl], ALU.mult))
                                    dve.wait_ge(s_free, l * SLOTS + N * 16 + 4 * q + 4)
                                    dve.tensor_tensor(diag[:, q % 2],
                                                      ident.unsqueeze(1).to_broadcast([P, BATCH, P]),
                                                      wt[:, y, sl].unsqueeze(2).to_broadcast([P, BATCH, P]),
                                                      ALU.mult).then_inc(s_diag, 1)
                                    if q == 0:
                                        find_rows(1 - y)
                                    elif q == 1:
                                        set_gate(1 - y, sel0 + n + 2)
                                        choose_first(y, sel0 + n + 3)
                                    elif q == 2:
                                        choose_second()
                                    else:
                                        choose_pairs()
                            next_round()
                    step(dve.tensor_scalar(row0, row0, float(KEYS * KEYS), None, ALU.add))
                    next_round()


                @block.tensor
                def _(pe):
                    pe.wait_ge(s_pool, 5)

                    def fill(*name):
                        n = FILL_NO[name]
                        if n >= 2:
                            pe.wait_ge(drained[n % 2], n // 2)
                        return bank[n % 2]

                    def full(ins, *name):
                        ins.then_inc(filled[FILL_NO[name] % 2], 1)

                    def parts(*name):
                        m = SPLIT_NO[name]
                        pe.wait_ge(s_wlo, m + 1)
                        return w_hi[:, m % PARTS], w_lo[:, m % PARTS]

                    def product(kind, j, x, ks=range(NK), ready=None):
                        z = fill(kind, j)
                        wh, wl = (w.rearrange("p (k c) -> p k c", k=NK) for w in parts(kind, j))
                        for k in ks:
                            if ready:
                                pe.wait_ge(ready[0], ready[1] + k + 1)
                            pe.matmul(z, wh[:, k], x[0][:, k], start=(k == 0), stop=False)
                            pe.matmul(z, wh[:, k], x[1][:, k], start=False, stop=False)
                            ins = pe.matmul(z, wl[:, k], x[0][:, k], start=False, stop=(k == NK - 1))
                        if ks[-1] == NK - 1:
                            full(ins, kind, j)

                    def product_a(j):
                        z, w = fill("a", j), loaded(pe, ("a", j)).rearrange("p (k c) -> p k c", k=NK)
                        for k in range(NK):
                            ins = pe.matmul(z, w[:, k], uT[:, k], start=(k == 0), stop=(k == NK - 1))
                        full(ins, "a", j)

                    def turn(name, i, pieces):
                        z = fill(name, i)
                        for m, part in enumerate(pieces):
                            ins = pe.transpose(z[:, m * P:(m + 1) * P], part, ident)
                        full(ins, name, i)

                    def turn_normed():
                        for k in range(NK):
                            for b in range(NB):
                                ins = pe.matmul(ps[k][:, b * P:(b + 1) * P], X[:, b, k * P:(k + 1) * P], rdiag[:, b],
                                                start=True, stop=True)
                            ins.then_inc(s_tfull, 1)

                    pe.wait_ge(s_rdiag, 1)
                    turn_normed()
                    for kind in ("v", "xm", "u"):
                        for j in range(NK):
                            product(kind, j, hT, ready=(s_tlow, 0) if (kind, j) == ("v", 0) else None)
                    for i in range(2 * NB):
                        b, half = i // 2, i % 2
                        turn("vr", i, [vT[:, 4 * half + m, b * P:(b + 1) * P] for m in range(4)])
                    for j in range(NK):
                        product("o", j, hT)
                    pe.wait_ge(s_vs, NB)
                    pe.wait_ge(s_par, 64)
                    for g in range(NK):
                        z = fill("mix", g)
                        for b in range(NB):
                            ins = pe.matmul(z[:, b * P:(b + 1) * P], v_rows[:, b, g * P:(g + 1) * P], wsT[:, g],
                                            start=True, stop=True)
                        full(ins, "mix", g)
                    for kind in ("ga", "gb"):
                        for j in range(NK):
                            product(kind, j, hT)
                    pe.wait_ge(s_xc, NK)
                    z = fill("gates", 0)
                    for k in range(NK):
                        ins = pe.matmul(z, wg[:, k], xcT[:, k], start=(k == 0), stop=(k == NK - 1))
                    full(ins, "gates", 0)

                    def qkv(h):
                        pe.wait_ge(s_qkvw, 16 * (h + 1))
                        for m, (w, dst) in enumerate((("q", qs), ("k", ks))):
                            for e in range(2):
                                z = fill(f"{w}{e}", h)
                                for c in range(2):
                                    ins = pe.matmul(z[:, :], WQKV[:, m, c, e * P:(e + 1) * P], xcT[:, 2 * h + c],
                                                    start=(c == 0), stop=(c == 1))
                                full(ins, f"{w}{e}", h)
                        for i in range(2):
                            z = fill(f"v{i}", h)
                            for b in range(2):
                                t0 = 2 + (2 * i + b) * P
                                for c in range(2):
                                    ins = pe.matmul(z[:, b * DH:(b + 1) * DH], xmT[:, 2 * h + c, t0:t0 + P],
                                                    WQKV[:, 2, c, :], start=(c == 0), stop=(c == 1))
                            full(ins, f"v{i}", h)

                    def head_turned(h):
                        pe.wait_ge(s_hn, h + 1)
                        pe.wait_ge(s_arg, 8 * min(h + 2, NH))
                        for e in range(2):
                            for b in range(NB):
                                ins = pe.transpose(ps_a[e][:, b * P:(b + 1) * P], h_head[:, b, e * P:(e + 1) * P],
                                                   ident)
                            ins.then_inc(s_hdfull, 1)

                    def stabilisers(h):
                        if h >= 2:
                            pe.wait_ge(s_hdout, 2 * (h - 1))
                        elif h:
                            pe.wait_ge(s_arg, 8 * h)
                        for d in range(2):
                            ins = pe.matmul(ps_a[d][:, :], sel[0:NH, h], g_f[:, d], start=True, stop=True)
                        ins.then_inc(s_afull, 1)

                    qkv(0)
                    pe.wait_ge(s_ya, NK)
                    product_a(0)
                    product_a(1)
                    z = fill("cols", 0)
                    pe.wait_ge(s_rows, 1)
                    pe.wait_ge(s_em, 1)
                    for i, g in enumerate((g_i, g_t)):
                        for d in range(2):
                            for b in range(NB):
                                o = ((i * 2 + d) * NB + b) * NH
                                ins = pe.transpose(z[:, o:o + NH], g[:, d, b * P:(b + 1) * P], ident[0:NH, 0:NH])
                    full(ins, "cols", 0)
                    pe.wait_ge(s_one, 4)
                    stabilisers(0)
                    for h in range(NH):
                        for n in ("q0", "q1", "k0", "k1", "v0", "v1"):
                            is_drained(pe, n, h)
                        for c in range(NB):
                            i = NB * h + c
                            if i >= 2:
                                pe.wait_ge(s_p, 2 * (i - 1))
                            for e in range(2):
                                ins = pe.matmul(ps_s[c % 2][:, :], ks[:, e, c * P:(c + 1) * P], qs[:, e],
                                                start=(e == 0), stop=(e == 1))
                            ins.then_inc(s_sfull, 1)
                        if h:
                            head_turned(h - 1)
                        if h + 1 < NH:
                            qkv(h + 1)
                        pe.wait_ge(s_p, 8 * (h + 1))
                        for i in range(2 * NB):
                            d, b = i // NB, i % NB
                            if i in (0, 1):
                                if h:
                                    pe.wait_ge(s_hsum, 4 * h - 1 + i)
                            elif i < 6:
                                pe.wait_ge(s_nfree, 4 * h + i - 1)
                            else:
                                pe.wait_ge(s_hsum, 4 * h + i - 5)
                            srcs = range(0, b + 1) if d == 0 else range(b, NB)
                            for c in srcs:
                                w, t0, n = attn(d, c)
                                ins = pe.matmul(ps_n[i % 2][:, 0:VA], w[:, b * P - t0:(b + 1) * P - t0],
                                                vaug[h % 2][:, c], start=(c == srcs[0]), stop=(c == srcs[-1]))
                            ins.then_inc(s_nfull, 1)
                        if h + 1 < NH:
                            stabilisers(h + 1)
                            product_a(2 * h + 2)
                            product_a(2 * h + 3)
                    for j in range(2):
                        product("b", j, ybT, range(NK - 2), (s_yb, 0))
                    head_turned(NH - 1)
                    for j in range(2):
                        product("b", j, ybT, range(NK - 2, NK), (s_yb, 0))
                    for j in range(2, NK):
                        product("b", j, ybT)
                    for j in range(NK):
                        half, m = j // 4, j % 4
                        if not half:
                            pe.wait_ge(s_ya, NK + 2 * (m + 1))
                        wh, wl = (w.rearrange("p (k c) -> p k c", k=2) for w in parts("wo", j))
                        for b in range(NB):
                            if half and m == 0:
                                pe.wait_ge(s_wofree, b + 1)
                            for i in range(2):
                                k = 2 * m + i
                                xh, xl = (t[:, k, b * P:(b + 1) * P] for t in mT)
                                end = m == 3 and i == 1
                                pe.matmul(ps[4 + b], xh, wh[:, i], start=(m == 0 and i == 0), stop=False)
                                pe.matmul(ps[4 + b], xh, wl[:, i], start=False, stop=False)
                                ins = pe.matmul(ps[4 + b], xl, wh[:, i], start=False, stop=end)
                            if m == 3:
                                ins.then_inc(s_wosum, 1)
                        if m < 3:
                            ins.then_inc(s_wotile, 1)
                    pe.wait_ge(s_rdiag, 2)
                    turn_normed()
                    pe.sem_inc(s_free, SLOTS // 2)

                    sel0 = l * (NSEL + 2)

                    def key_scores(y, head, staged, copied):
                        if copied is not None:
                            pe.wait_ge(s_cv, copied)
                        pe.wait_ge(s_q, staged)
                        for h in range(2):
                            ins = pe.matmul(ps_k[y][:, h * KEYS:(h + 1) * KEYS], q_now[:, y, h],
                                            keysT[:, head * 2 + h], start=True, stop=True)
                        ins.then_inc(s_sc, 1)

                    pe.wait_ge(s_keys, 16)
                    for j in range(2 * PH):
                        product("pq", j, xnT, ready=(s_tlow, NK) if j == 0 else None)
                        if j in SCORES_AT:
                            m = SCORES_AT.index(j)
                            key_scores(m, m, sel0 + m + 1, None)
                    is_drained(pe, "pq", 2 * PH - 2)
                    is_drained(pe, "pq", 2 * PH - 1)
                    pe.sem_inc(s_free, SLOTS // 2)
                    with pe.Fori(0, NB) as b:
                        pe.wait_ge(s_vfree, 2 * (l * NB + b) + 2)
                        for half in range(2):
                            pe.matmul(ps_v[half], ident, X[:, b, half * S:(half + 1) * S], start=True, stop=False,
                                      skip_group_check=True)
                        with pe.Fori(0, PH // 2) as hp:
                            for y in range(2):
                                n, N = numbers(b, hp, y)
                                key_scores(y, (hp * 2 + y + 2) % PH, sel0 + n + 3, sel0 + n + 1)
                                for q in range(4):
                                    pe.wait_ge(s_diag, N * 4 + q + 1)
                                    for k in range(4):
                                        for half in range(2):
                                            ins = pe.matmul(ps_v[half], diag[:, q % 2, k],
                                                            slot[:, (4 * q + k) % SLOTS, 1, half * S:(half + 1) * S],
                                                            start=False, stop=False, skip_group_check=True)
                                        ins.then_inc(s_free, 1)

            nc.all_engine_barrier()
            with nc.Block() as block:
                @block.sync
                def _(sp):
                    lo, hi = filled[0].num, s_clear_last.num
                    sp.sem_clear(range(lo, hi + 1))

        with nc.Block() as block:
            @block.sync
            def _(sp):
                sp.dma_start(ffg, fin_g.to_broadcast([P, D])).then_inc(s_x, 16)
                for b in range(NB):
                    sp.wait_ge(s_fin, b + 1)
                    sp.dma_start(out[b * P:(b + 1) * P, :], xn[:, b]).then_inc(s_out, 16)
                sp.wait_ge(s_out, 16 * NB)

            @block.scalar
            def _(act):
                for b in range(NB):
                    act.activation(h_rows[:, b], X[:, b], ACT.Square, accum_out=ss4[:, b:b + 1]).then_inc(s_fsq, 1)
                    act.wait_ge(s_fsq, b + 1)
                    act.activation(ss4[:, b:b + 1], ss4[:, b:b + 1], ACT.Sqrt, bias=eps, scale=1.0 / D)\
                       .then_inc(s_fstd, 1)

            @block.vector
            def _(dve):
                for b in range(NB):
                    dve.wait_ge(s_fstd, b + 1)
                    dve.reciprocal(ss4[:, b:b + 1], ss4[:, b:b + 1]).then_inc(s_frs, 1)
                    dve.wait_ge(s_frs, b + 1)
                    if b == 0:
                        dve.wait_ge(s_x, 32)
                    dve.scalar_tensor_tensor(xn[:, b], X[:, b], ss4[:, b:b + 1], ffg, ALU.mult, ALU.mult)\
                       .then_inc(s_fin, 1)


_PARAMS = ("norm_mix_g", "gm_norm_g", "ml_conv_b", "ml_head_g", "ml_skip", "norm_ffn_g")


def _launch_arrays(i):
    import numpy as np

    a = {k: np.asarray(v) for k, v in i.items()}
    f = np.float32

    def by_feature(v):
        return v.reshape(L, NK, P).transpose(0, 2, 1)

    def by_tile(w):
        n = w.shape[2] // P
        return w.reshape(L, NK, P, n, P).transpose(0, 3, 2, 1, 4)

    par = np.zeros((L, P, NPAR), f)
    for n, name in enumerate(_PARAMS):
        par[:, :, 8 * n:8 * n + 8] = by_feature(a[name].reshape(L, D))
    cw = a["ml_conv_w"].reshape(L, CONV, NK, P).transpose(0, 3, 2, 1)
    par[:, :, P_CW:P_BG] = cw.reshape(L, P, NK * CONV)
    par[:, 0:NH, P_BG:] = a["ml_b_gate"].reshape(L, 4, NH).transpose(0, 2, 1)
    wg = np.zeros((L, D, P), f)
    for t in range(4):
        wg[:, :, 32 * t:32 * t + NH] = a["ml_w_gate"][:, :, NH * t:NH * (t + 1)]
    qkv = np.stack([a[n].reshape(L, NH, 2, P, DH) for n in ("ml_w_q", "ml_w_k", "ml_w_v")], axis=3)
    out = {
        "x_in": a["x"].reshape(S, D),
        "par": par,
        "bs": a["gm_b_s"],
        "ws": a["gm_w_s"].transpose(0, 3, 1, 2),
        "w_in": by_tile(a["w_in"]),
        "w_qkv": qkv.transpose(0, 1, 4, 3, 2, 5),
        "w_g": wg.reshape(L, NK, P, P).transpose(0, 2, 1, 3),
        "w_a": by_tile(a["w_branch_a"]),
        "w_b": by_tile(a["w_branch_b"]),
        "w_o": a["w_out"].reshape(L, 4, 2, P, 2, S).transpose(0, 4, 1, 3, 2, 5).reshape(L, 8, P, NK, P),
        "ffn_g": a["norm_ffn_g"],
        "w_pq": by_tile(a["peer_w_query"]),
        "keys": a["peer_sub_keys"].reshape(L, 2 * PH, KEYS, P).transpose(0, 3, 1, 2),
        "uv": np.concatenate([a["peer_u"], a["peer_v"]], axis=2).reshape(L * KEYS * KEYS, 2 * D),
        "fin_g": a["final_g"].reshape(1, D),
    }
    return {k: np.ascontiguousarray(v) for k, v in out.items()}


def kernel(**inputs):
    import concourse.bacc as bacc
    from concourse.bass_utils import run_bass_kernel_spmd as run

    nc = bacc.Bacc("TRN2", target_bir_lowering=False, num_devices=1)
    arrays = _launch_arrays(inputs)
    aps = {n: nc.dram_tensor(f"in_{n}", v.shape, mybir.dt.from_np(v.dtype), kind="ExternalInput").ap()
           for n, v in arrays.items()}
    out = nc.dram_tensor("out", (S, D), F32, kind="ExternalOutput").ap()
    build(nc, out=out, **aps)
    r = run(nc, [{f"in_{n}": v for n, v in arrays.items()}], core_ids=[0])
    return r.results[0]["out"].reshape(1, S, D)
```

```python
from contextlib import ExitStack

import concourse.bass as bass
from concourse import mybir

ALU = mybir.AluOpType
ACT = mybir.ActivationFunctionType
AX = mybir.AxisListType
F32 = mybir.dt.float32
F32R = mybir.dt.float32r
U32 = mybir.dt.uint32

P = 128
S = 512
D = 1024
NB = S // P
NK = D // P
L = 2
NH = 4
DH = D // NH
CONV = 5
PH = 8
KEYS = 128
TOPK = 16
EPS = 1e-6
LOWEST = -3.0e38
RAW, PARTS = 2, 3
SLOTS = 8
BATCH = 2
NQ = TOPK // BATCH
SIZE = 53200
EARLY = 6
LATE = 2 * PH - EARLY
NSEL = NB * PH

(P_MIXG, P_GMG, P_CB, P_HG, P_SK) = (8 * i for i in range(5))
P_FFG = 40
P_CW = 48
P_BG = P_CW + 8 * CONV
NPAR = P_BG + 4

QKV = ("q0", "q1", "k0", "k1", "v0", "v1")


def _each(*kinds, n=NK):
    return [(kind, j) for kind in kinds for j in range(n)]


FILLS = (_each("xm", "u") + [(n, j) for j in range(NK) for n in ("o", "mix")] + _each("ga", "gb")
         + [("gates", 0)] + [(n, 0) for n in QKV] + [("a", 0), ("a", 1), ("cols", 0)])
for _h in range(NH - 1):
    FILLS += [(n, _h + 1) for n in QKV] + [("a", 2 * _h + 2), ("a", 2 * _h + 3)]
FILLS += _each("b") + _each("pq", n=EARLY)
AHEAD = 6 * NK + PARTS
SCORES_AT = (2, 4)
FILL_NO = {name: n for n, name in enumerate(FILLS)}

TILES = (_each("v", "xm", "u", "o", "ga", "gb") + _each("b", n=PARTS) + _each("a")
         + _each("b")[PARTS:] + _each("wo") + _each("pq", n=EARLY))
SPLIT = [t for t in TILES if t[0] != "a"]
SPLIT_NO = {name: n for n, name in enumerate(SPLIT)}
TILE_NO = {name: n for n, name in enumerate(TILES)}
SECTION = {"u": 0, "xm": 1, "o": 2, "ga": 3, "gb": 4}


class Own:

    def __init__(self, eng):
        self.eng, self.n = eng, {}

    def tell(self, ins, sem):
        ins.then_inc(sem, 1)
        self.n[sem.name] = self.n.get(sem.name, 0) + 1

    def done(self, sem):
        self.eng.wait_ge(sem, self.n[sem.name])

    def link(self, ins, sem):
        self.tell(ins, sem)
        self.done(sem)

    def forget(self, sem):
        self.n[sem.name] = 0


def build(nc, x_in, par, bs, ws, w_in, w_v, w_qkv, w_g, w_a, w_b, w_o, ffn_g, w_pq, keys, uv, fin_g, out):
    ctx = ExitStack()
    with ctx:
        ctx.enter_context(nc.sbuf_tensor("reserved", [P, SIZE], F32))
        base = nc.sbuf_base - 4 * SIZE
        at = [0]

        def place(name, n, start, dtype=F32):
            return nc.alloc_sbuf_tensor_at(name, [P, n], dtype, offset=base + 4 * start)[:, :]

        def take(name, n):
            start, at[0] = at[0], at[0] + -(-n // 8) * 8
            return place(name, n, start)

        def rows(t):
            return t.rearrange("p (b d) -> p b d", b=NB)

        def chunks(t, n=NK):
            return t.rearrange("p (k t) -> p k t", k=n)

        X = rows(take("X", NB * D))
        at_R1 = at[0]
        R1 = take("R1", NK * S + 16)
        R2 = take("R2", NK * S)
        at_R3 = at[0]
        R3 = take("R3", NK * S)
        at_R4 = at[0]
        R4 = take("R4", NK * (S + 4))
        at_R5 = at[0]
        R5 = take("R5", NK * S)
        at_R6 = at[0]
        R6 = take("R6", NK * S)
        at_R7 = at[0]
        R7 = take("R7", NK * S)
        at_RW = at[0]
        RW = take("RW", (RAW + 2 * PARTS) * D)
        at_WQKV = at[0]
        WQKV = take("WQKV", 3 * 2 * DH).rearrange("p (m c e) -> p m c e", m=3, c=2)
        at_PW = at[0]
        PW = take("PW", 3 * D)
        HR = take("HR", NB * DH)
        at_G = at[0]
        G = [take(f"G{i}", 2 * S) for i in range(5)]
        sg = take("sg", S)
        sel = take("sel", NH * P).rearrange("p (h m) -> p h m", h=NH)
        ident = take("ident", P)
        prm = take("prm", NPAR)
        cols = take("cols", 64).rearrange("p (i d b h) -> p i d b h", i=2, d=2, b=NB)
        small = take("small", 64)
        unused = small[:, 48:49]
        eps = small[:, 61:62]
        row0 = small[:, 60:61]
        assert at[0] <= SIZE, at

        xcT = chunks(R7)
        h_rows, v_rows, gbT = rows(R2), rows(R2), chunks(R2)
        uT, oT = chunks(R3), chunks(R5)
        xmT = R4.rearrange("p (k t) -> p k t", k=NK)
        gaT = chunks(R6)
        raw = RW[:, 0:RAW * D].rearrange("p (r n) -> p r n", r=RAW)
        w_hi, w_lo = (place(name, PARTS * D, at_RW + (RAW + i * PARTS) * D, F32R)
                      .rearrange("p (r n) -> p r n", r=PARTS) for i, name in enumerate(("w_hi", "w_lo")))
        hT, ybT, mT, xnT = ([chunks(place(f"{name}_{part}", NK * S, start, F32R))
                             for part, start in zip(("hi", "lo"), starts)]
                            for name, starts in (("hT", (at_R1, at_G)), ("ybT", (at_R5, at_R7)),
                                                 ("mT", (at_R3, at_R4)), ("xnT", (at_R1, at_G))))
        wsT = PW[:, 0:D].rearrange("p (g t) -> p g t", g=NK)
        bsb = PW[:, D:2 * D].rearrange("p (g t) -> p g t", g=NK)
        wg = PW[:, 2 * D:3 * D].rearrange("p (k m) -> p k m", k=NK)
        qs, ks = (R1[:, i * 2 * S:(i + 1) * 2 * S].rearrange("p (c t) -> p c t", c=2) for i in range(2))
        VA = DH + 1
        vaug = [R1[:, 4 * S + i * NB * VA:4 * S + (i + 1) * NB * VA].rearrange("p (b e) -> p b e", b=NB)
                for i in range(2)]
        h_head = HR.rearrange("p (b e) -> p b e", b=NB)
        tmp = HR[:, 0:S]
        g_i, g_f, g_t, g_F, g_M = (g[0:NH].rearrange("p (d t) -> p d t", d=2) for g in G)
        junk = G[0]
        ffg = place("ffn_gain", D, at_WQKV)
        rdiag = sg.rearrange("p (b m) -> p b m", b=NB)
        work = place("work", NK * S, at_PW)
        late_raw, late_lo = G[4], place("late_lo", D, at_G + 8 * S, F32R)
        late_hi = place("late_hi", D, at_WQKV, F32R)
        ss1, ss2, ss3, ss4 = (small[:, 4 * i:4 * i + 4] for i in range(4))
        den = small[:, 16:24]
        hss, ss5 = small[:, 24:28], small[:, 28:32]
        iota16 = small[:, 32:48]

        def attn(d, c):
            n = (NB - c) * P if d == 0 else (c + 1) * P
            off = sum((NB - i) * P for i in range(c)) if d == 0 else 10 * P + sum((i + 1) * P for i in range(c))
            return PW[:, off:off + n], (c * P if d == 0 else 0), n

        xn = rows(R2)
        q_flat = place("queries", 2 * PH * S, at_R3)
        qT = q_flat.rearrange("p (b m t) -> p b m t", b=NB, m=2 * PH)
        q_heads = q_flat.rearrange("p (n c) -> p n c", n=NSEL)
        slot = place("slots", SLOTS * 2 * D, at_R6).rearrange("p (r w d) -> p r w d", r=SLOTS, w=2)
        keysT = R5[:, 0:2 * PH * KEYS].rearrange("p (m k) -> p m k", m=2 * PH)
        q_now = R5[:, 2048:2560].rearrange("p (y h t) -> p y h t", y=2, h=2)
        x_now = R5[:, 2560:3584]
        diag = work[:, 0:SLOTS * P].rearrange("p (r m) -> p r m", r=SLOTS)
        o_ = [SLOTS * P]

        def piece(n):
            o_[0] += n
            return work[:, o_[0] - n:o_[0]]
        sc2 = piece(256).rearrange("p (h k) -> p h k", h=2)
        sc2r = piece(KEYS)
        cand, cand2 = piece(256), piece(256)
        onehot, picked = (piece(512).rearrange("p (h k j) -> p h k j", h=2, k=TOPK) for _ in range(2))
        sv = piece(32).rearrange("p (h k) -> p h k", h=2)
        si = piece(32).bitcast(U32).rearrange("p (h k) -> p h k", h=2)
        cv = piece(16)
        ci = piece(16).bitcast(U32)
        cab = piece(32).bitcast(U32).rearrange("p (h k) -> p h k", h=2)
        pick = piece(32).rearrange("p (h k) -> p h k", h=2)
        idx = piece(32).bitcast(U32).rearrange("p (y k) -> p y k", y=2)
        ex = piece(16)
        gate = piece(32).rearrange("p (y k) -> p y k", y=2)
        esum, ncv, rin = piece(1), piece(1), piece(1)
        dots = piece(32).rearrange("p (y k) -> p y k", y=2)
        acts = piece(32).rearrange("p (y k) -> p y k", y=2)
        wt = piece(32).rearrange("p (y k) -> p y k", y=2)
        assert o_[0] <= NK * S

        ps = [ctx.enter_context(nc.psum_tensor(f"bank{i}", [P, S], F32))[:, :] for i in range(8)]
        bank = ps[0:2]
        ps_s = ps[2:4]
        ps_a = ps[4:6]
        ps_n = ps[6:8]
        ps_v = ps[0:2]
        ps_k = ps[2:4]
        ps_q = ps[4:6]

        def sem(name):
            return ctx.enter_context(nc.semaphore(name))

        s_x, s_out, s_pool = sem("x_loaded"), sem("out_stored"), sem("pool_constants")
        filled = [sem(f"bank_filled{i}") for i in range(2)]
        drained = [sem(f"bank_drained{i}") for i in range(2)]
        s_par, s_ffg, s_keys = sem("params_loaded"), sem("ffn_gain_loaded"), sem("keys_loaded")
        s_w = [sem(f"weights_loaded{i}") for i in range(RAW)]
        s_whi, s_wlo = sem("weights_hi"), sem("weights_lo")
        s_hhi, s_ybhi, s_mval, s_mhi, s_xhi = sem("h_hi"), sem("yb_hi"), sem("merged"), sem("merged_hi"), sem("x_hi")
        s_ybval = sem("yb_value")
        s_tfull, s_tlow = sem("turned"), sem("turned_lo")
        s_hdfull, s_hdout = sem("head_turned"), sem("head_taken")
        s_sg = sem("conv_sigmoid")
        s_wotile, s_wosum, s_wofree = sem("wo_tile_used"), sem("wo_summed"), sem("wo_added")
        s_vtile, s_vsum, s_vout = sem("v_tile_used"), sem("v_summed"), sem("v_rows_out")
        s_qkvw = sem("qkv_weights_loaded")
        s_a, s_d = sem("act_step"), sem("dve_step")
        s_sq, s_sqd, s_sqv, s_sqx = (sem(n) for n in ("h_squares", "h_squares_dve", "v_squares", "x_squares"))
        s_rdiag, s_vs, s_xr = sem("rstd_diagonal"), sem("v_rows_scaled"), sem("x_rows_ready")
        s_late, s_latehi, s_latelo = sem("late_tile_loaded"), sem("late_tile_hi"), sem("late_tile_lo")
        s_latefull, s_latefree = sem("late_queries_full"), sem("late_queries_out")
        s_sqsum = sem("x_squares_summed")
        s_ya, s_yb = sem("ya_ready"), sem("yb_ready")
        s_conv, s_xc = sem("conv_done"), sem("xc_ready")
        s_gin, s_nabs, s_ln = sem("gates_in"), sem("gates_negabs"), sem("gates_ln")
        s_fm, s_rows = sem("gates_stabiliser"), sem("gates_rows_ready")
        s_em = sem("gates_em_ready")
        s_afull = sem("a_full")
        s_arg, s_exp, s_mask, s_p = sem("attn_arg"), sem("attn_exp"), sem("attn_masked"), sem("attn_ready")
        s_sfull = sem("scores_full")
        s_nfull, s_nfree = sem("num_full"), sem("num_free")
        s_hsum, s_hsq, s_hn = sem("head_summed"), sem("head_squares"), sem("head_normed")
        s_xs = sem("xc_skip")
        s_one = sem("vaug_ones")
        s_table, s_std, s_rstd = sem("sqrt_table"), sem("std_ready"), sem("rstd_ready")
        s_clear_last = sem("layer_end")
        s_gather = [sem(f"gathered{i}") for i in range(SLOTS)]
        s_free = sem("slots_free")
        s_idx = sem("indices_ready")
        s_dot, s_act, s_diag = sem("dots_ready"), sem("gelu_ready"), sem("diag_ready")
        s_q, s_sc = sem("query_staged"), sem("key_scores_ready")
        s_cv, s_ex = sem("top_ready"), sem("exp_ready")
        s_vfree = sem("block_added")
        s_ps = sem("peer_dve_step")
        s_vfree0 = sem("row0_set")
        s_fsq, s_fin = sem("final_squares"), sem("final_ready")
        s_fstd, s_frs = sem("final_std"), sem("final_rstd")

        def is_filled(eng, *name):
            n = FILL_NO[name]
            eng.wait_ge(filled[n % 2], n // 2 + 1)
            return bank[n % 2]

        def drain(ins, *name):
            ins.then_inc(drained[FILL_NO[name] % 2], 1)

        def is_drained(eng, *name):
            n = FILL_NO[name]
            eng.wait_ge(drained[n % 2], n // 2 + 1)

        def loaded(eng, name):
            n = TILE_NO[name]
            eng.wait_ge(s_w[n % RAW], 16 * (n // RAW + 1))
            return raw[:, n % RAW]

        def is_multiplied(eng, m):
            kind, j = SPLIT[m]
            if kind in ("v", "wo"):
                half, m4 = j // 4, j % 4
                tile, total = (s_vtile, s_vsum) if kind == "v" else (s_wotile, s_wosum)
                if m4 == 3:
                    eng.wait_ge(total, NB * (half + 1))
                else:
                    eng.wait_ge(tile, 3 * half + m4 + 1)
            else:
                is_filled(eng, kind, j)

        with nc.Block() as block:
            @block.sync
            def _(sp):
                sp.dma_start(X, x_in.rearrange("(b p) d -> p b d", p=P)).then_inc(s_x, 16)

            @block.gpsimd
            def _(pool):
                pool.memset(ident, 0.0).then_inc(s_pool, 1)
                pool.memset(sel, 1.0).then_inc(s_pool, 1)
                pool.wait_ge(s_pool, 2)
                pool.affine_select(out=ident, in_=ident, compare_op=ALU.not_equal, fill=1.0, base=0,
                                   pattern=[[-1, P]], channel_multiplier=1).then_inc(s_pool, 1)
                pool.affine_select(out=sel, in_=sel, compare_op=ALU.is_equal, fill=0.0, base=0,
                                   pattern=[[-1, NH], [0, P]], channel_multiplier=1).then_inc(s_pool, 1)
                pool.iota(iota16, [[1, TOPK]], base=0, channel_multiplier=0,
                          allow_small_or_imprecise_dtypes=True).then_inc(s_pool, 1)
                pool.wait_ge(s_pool, 5)

            @block.tensor
            def _(pe):
                pe.sem_inc(s_vfree, 2)

            @block.vector
            def _(dve):
                dve.memset(row0, 0.0).then_inc(s_vfree0, 1)
                dve.memset(eps, EPS).then_inc(s_vfree0, 1)
                dve.wait_ge(s_vfree0, 2)
                dve.wait_ge(s_x, 16)

        with nc.Fori(0, L) as l:
            def numbers(b, hp, y):
                n = b * PH + hp * 2 + y
                return n, l * NSEL + n

            with nc.Block() as block:
                @block.sync
                def _(sp):
                    lay = bass.ds(l, 1)
                    sp.dma_start(prm, par[lay].rearrange("l p c -> (l p) c")).then_inc(s_par, 16)
                    sp.dma_start(wsT, ws[lay].rearrange("l p g t -> (l p) g t")).then_inc(s_par, 16)
                    sp.dma_start(bsb, bs[lay].rearrange("l g t -> l (g t)").to_broadcast([P, D])
                                 .rearrange("p (g t) -> p g t", g=NK)).then_inc(s_par, 16)
                    sp.dma_start(wg, w_g[lay].rearrange("l p k m -> (l p) k m")).then_inc(s_par, 16)

                    def load_qkv(h):
                        if h >= 1:
                            is_filled(sp, "v1", h - 1)
                        sp.dma_start(WQKV, w_qkv[lay, h].rearrange("l p m c e -> (l p) m c e"))\
                          .then_inc(s_qkvw, 16)

                    for n, (kind, j) in enumerate(TILES):
                        if kind == "ga" and j == 0:
                            load_qkv(0)
                        if kind == "a" and j >= 2 and j % 2 == 0:
                            load_qkv(j // 2)
                        if n >= RAW:
                            old = TILES[n - RAW]
                            if old[0] == "a":
                                is_filled(sp, *old)
                            else:
                                sp.wait_ge(s_wlo, SPLIT_NO[old] + 1)
                        if kind == "pq" and j == 0:
                            is_filled(sp, "b", NK - 1)
                            sp.dma_start(keysT, keys[lay].rearrange("l p m k -> (l p) m k")).then_inc(s_keys, 16)
                        if kind in SECTION:
                            src = w_in[lay, SECTION[kind] * NK + j]
                        else:
                            src = {"v": w_v, "wo": w_o, "a": w_a, "b": w_b, "pq": w_pq}[kind][lay, j]
                        sp.dma_start(raw[:, n % RAW], src.rearrange("l p k c -> (l p) (k c)"))\
                          .then_inc(s_w[n % RAW], 16)
                        if kind == "a" and j == NK - 1:
                            is_filled(sp, "v1", NH - 1)
                            sp.dma_start(ffg, ffn_g[lay].to_broadcast([P, D])).then_inc(s_ffg, 16)
                    for i in range(LATE):
                        if i:
                            sp.wait_ge(s_latefull, i)
                        sp.dma_start(late_raw, w_pq[lay, EARLY + i].rearrange("l p k c -> (l p) (k c)"))\
                          .then_inc(s_late, 16)

                @block.gpsimd
                def _(pool):
                    def lows(kinds):
                        for m, name in enumerate(SPLIT):
                            if name in kinds:
                                pool.wait_ge(s_whi, m + 1)
                                w = loaded(pool, name)
                                pool.tensor_tensor(w_lo[:, m % PARTS], w, w_hi[:, m % PARTS].bitcast(F32),
                                                   ALU.subtract).then_inc(s_wlo, 1)

                    pool.memset(xmT[:, :, 0:2], 0.0).then_inc(s_one, 1)
                    pool.memset(xmT[:, :, S + 2:S + 4], 0.0).then_inc(s_one, 1)
                    lows(SPLIT[:AHEAD])
                    is_filled(pool, "gb", NK - 1)
                    for i in range(2):
                        pool.memset(vaug[i][:, :, DH:VA], 1.0).then_inc(s_one, 1)
                    for h in range(NH):
                        for c in range(NB):
                            for d in range(2):
                                w, t0, n = attn(d, c)
                                o = 0 if d == 0 else c * P
                                sgn = 1 if d == 0 else -1
                                pool.wait_ge(s_exp, 8 * h + 2 * c + d + 1)
                                pool.affine_select(out=w[:, o:o + P], in_=w[:, o:o + P], compare_op=ALU.is_ge,
                                                   fill=0.0, base=0, pattern=[[sgn, P]],
                                                   channel_multiplier=-sgn).then_inc(s_mask, 1)
                    lows(SPLIT[AHEAD:])

                    want_free, want_idx = pool.alloc_register("want_free"), pool.alloc_register("want_idx")
                    pool.reg_mov(want_free, l * (NSEL * TOPK + SLOTS) + 1)
                    pool.reg_mov(want_idx, l * (NSEL + 1) + 1)

                    def gathers(y, ks):
                        for k in ks:
                            pool.wait_ge(s_free, want_free)
                            pool.reg_add(want_free, want_free, 1)
                            pool.indirect_dma_start(
                                out=slot[:, k % SLOTS].rearrange("p w d -> p (w d)"), out_offset=None, in_=uv,
                                in_offset=bass.IndirectOffsetOnAxis(ap=idx[:, y, k:k + 1], axis=0))\
                                .then_inc(s_gather[k % SLOTS], 16)

                    def late_low(i):
                        if i < LATE:
                            pool.wait_ge(s_latehi, i + 1)
                            pool.tensor_tensor(late_lo, late_raw, late_hi.bitcast(F32), ALU.subtract)\
                                .then_inc(s_latelo, 1)

                    for n in range(PH):
                        pool.wait_ge(s_idx, want_idx)
                        pool.reg_add(want_idx, want_idx, 1)
                        gathers(n % 2, range(TOPK // 2))
                        late_low(2 * n)
                        gathers(n % 2, range(TOPK // 2, TOPK))
                        late_low(2 * n + 1)
                    with pool.Fori(PH // 2, NSEL // 2) as pair:
                        for y in range(2):
                            pool.wait_ge(s_idx, want_idx)
                            pool.reg_add(want_idx, want_idx, 1)
                            gathers(y, range(TOPK))

                @block.scalar
                def _(act):
                    own = Own(act)

                    def std(ss, n):
                        act.activation(ss, ss, ACT.Sqrt, bias=eps, scale=1.0 / n).then_inc(s_std, 1)

                    def load_sqrt():
                        own.link(act.activation(unused, eps, ACT.Sqrt), s_table)

                    def prepare(m):
                        if m >= len(SPLIT):
                            return
                        w = loaded(act, SPLIT[m])
                        if m >= PARTS:
                            is_multiplied(act, m - PARTS)
                        act.activation(w_hi[:, m % PARTS], w, ACT.Copy).then_inc(s_whi, 1)

                    def section(kind, out, func):
                        for j in range(NK):
                            if SPLIT_NO[(kind, j)] + 2 < AHEAD:
                                prepare(SPLIT_NO[(kind, j)] + 2)
                            drain(act.activation(out(j), is_filled(act, kind, j), func), kind, j)

                    load_sqrt()
                    for b in range(NB // 2):
                        act.activation(h_rows[:, b], X[:, b], ACT.Square, accum_out=ss1[:, b:b + 1])\
                           .then_inc(s_sq, 1)
                    act.wait_ge(s_sq, NB // 2)
                    act.wait_ge(s_sqd, NB // 2)
                    std(ss1, D)
                    prepare(0)
                    prepare(1)
                    act.wait_ge(s_par, 64)
                    for k in range(NK):
                        act.wait_ge(s_tfull, k + 1)
                        act.activation(hT[0][:, k], ps[k], ACT.Copy,
                                       scale=prm[:, P_MIXG + k:P_MIXG + k + 1]).then_inc(s_hhi, 1)
                    for j in range(NK):
                        prepare(j + 2)
                        if j % 4 == 3:
                            half = j // 4
                            for b in range(NB):
                                act.wait_ge(s_vsum, half * NB + b + 1)
                                act.activation(v_rows[:, b, half * S:(half + 1) * S], ps[4 * half + b],
                                               ACT.Gelu_apprx_tanh).then_inc(s_vout, 1)
                    act.wait_ge(s_vout, 2 * NB)
                    for b in range(NB):
                        if b:
                            act.wait_ge(s_sqv, b)
                        act.activation(HR, v_rows[:, b], ACT.Square, accum_out=ss2[:, b:b + 1])\
                           .then_inc(s_sqv, 1)
                    act.wait_ge(s_sqv, NB)
                    std(ss2, D)
                    section("xm", lambda j: xmT[:, j, 2:S + 2], ACT.Copy)
                    section("u", lambda j: uT[:, j], ACT.Gelu_apprx_tanh)

                    def conv_sigmoid(j):
                        act.wait_ge(s_conv, j + 1)
                        if j:
                            act.wait_ge(s_xc, j)
                        act.activation(sg, xcT[:, j], ACT.Sigmoid).then_inc(s_sg, 1)

                    section("o", lambda j: oT[:, j], ACT.Sigmoid)
                    section("ga", lambda j: gaT[:, j], ACT.Sigmoid)
                    for j in range(NK):
                        conv_sigmoid(j)
                        prepare(SPLIT_NO[("gb", j)] + 2)
                        drain(act.activation(gbT[:, j], is_filled(act, "gb", j), ACT.Sigmoid), "gb", j)
                    prepare(AHEAD - 1)
                    z = is_filled(act, "gates", 0)
                    for i, (g, d) in enumerate(((g_i, 0), (g_f, 0), (g_i, 1), (g_f, 1))):
                        ins = act.activation(g[:, d], z[32 * i:32 * i + NH, :], ACT.Identity,
                                             bias=prm[0:NH, P_BG + i:P_BG + i + 1])
                        if i < 3:
                            ins.then_inc(s_gin, 1)
                        else:
                            drain(ins, "gates", 0)
                    act.wait_ge(s_nabs, 1)
                    act.activation(g_t, g_t, ACT.Exp).then_inc(s_a, 1)
                    act.wait_ge(s_a, 1)
                    act.activation(g_t, g_t, ACT.Ln, bias=1.0).then_inc(s_ln, 1)
                    def evacuate_qkv(h):
                        for e in range(2):
                            drain(act.activation(qs[:, e], is_filled(act, f"q{e}", h)[:, :], ACT.Copy), f"q{e}", h)
                        for e in range(2):
                            drain(act.activation(ks[:, e], is_filled(act, f"k{e}", h)[:, :], ACT.Copy,
                                                 scale=float(DH) ** -0.5), f"k{e}", h)
                        for i in range(2):
                            z = is_filled(act, f"v{i}", h)
                            drain(act.activation(vaug[h % 2][:, 2 * i:2 * i + 2, 0:DH],
                                                 z.rearrange("p (b e) -> p b e", b=2), ACT.Copy), f"v{i}", h)
                    evacuate_qkv(0)
                    act.wait_ge(s_fm, 1)
                    act.activation(g_t, g_t, ACT.Exp, scale=-1.0).then_inc(s_em, 1)
                    for h in range(NH):
                        for c in range(NB):
                            for d in range(2):
                                w, t0, n = attn(d, c)
                                act.wait_ge(s_arg, 8 * h + 2 * c + d + 1)
                                act.activation(w, w, ACT.Exp).then_inc(s_exp, 1)
                        if h + 1 < NH:
                            evacuate_qkv(h + 1)
                        for e in range(2):
                            f = 2 * h + e
                            act.activation(xcT[:, f], xcT[:, f], ACT.Copy,
                                           scale=prm[:, P_SK + f:P_SK + f + 1]).then_inc(s_xs, 1)
                        act.wait_ge(s_hsum, NB * (h + 1))
                        for b in range(NB):
                            if h or b:
                                act.wait_ge(s_hsq, NB * h + b)
                            act.activation(junk[:, 0:DH], h_head[:, b], ACT.Square,
                                           accum_out=hss[:, b:b + 1]).then_inc(s_hsq, 1)
                        act.wait_ge(s_hsq, NB * (h + 1))
                        std(hss, DH)

                    def hi(out, value, ready, n, sem_):
                        act.wait_ge(ready, n)
                        act.activation(out, value, ACT.Copy).then_inc(sem_, 1)

                    for j in range(NK):
                        prepare(SPLIT_NO[("b", j)] + PARTS)
                        if j:
                            hi(mT[0][:, j - 1], gaT[:, j - 1], s_mval, j, s_mhi)
                    hi(mT[0][:, NK - 1], gaT[:, NK - 1], s_mval, NK, s_mhi)

                    def squares(half):
                        for b in range(NB):
                            i = half * NB + b
                            act.wait_ge(s_wofree, i + 1)
                            act.activation(work[:, i * S:(i + 1) * S], X[:, b, half * S:(half + 1) * S], ACT.Square,
                                           accum_out=(ss3, ss5)[half][:, b:b + 1]).then_inc(s_sqx, 1)

                    for j in range(NK):
                        if j == NK // 2 + 1:
                            squares(0)
                            load_sqrt()
                        if j < NK - 1:
                            prepare(SPLIT_NO[("wo", j)] + PARTS)
                    squares(1)
                    act.wait_ge(s_sqsum, 1)
                    std(ss3, D)
                    prepare(SPLIT_NO[("wo", NK - 1)] + PARTS)
                    for k in range(NK):
                        act.wait_ge(s_tfull, NK + k + 1)
                        act.activation(xnT[0][:, k], ps[k], ACT.Copy,
                                       scale=prm[:, P_FFG + k:P_FFG + k + 1]).then_inc(s_xhi, 1)

                    def stage(m, y, before):
                        if before is not None:
                            act.wait_ge(s_sc, before)
                        act.activation(q_now[:, y].rearrange("p h t -> p (h t)"), q_heads[:, m], ACT.Copy)\
                           .then_inc(s_q, 1)

                    def exps(count):
                        act.wait_ge(s_cv, count)
                        act.activation(ex, cv, ACT.Exp, bias=ncv, accum_out=esum).then_inc(s_ex, 1)

                    sel0 = l * (NSEL + 2)
                    for j in range(EARLY):
                        prepare(SPLIT_NO[("pq", j)] + PARTS)
                        z = is_filled(act, "pq", j)
                        drain(act.activation(qT[:, :, j], z.rearrange("p (b t) -> p b t", b=NB), ACT.Copy), "pq", j)
                        if j in (1, 3):
                            is_drained(act, "pq", j - 1)
                            is_drained(act, "pq", j)
                            stage(j // 2, j // 2, None)
                    exps(sel0 + 1)
                    exps(sel0 + 2)
                    is_drained(act, "pq", EARLY - 2)
                    is_drained(act, "pq", EARLY - 1)

                    def gelus(N, y, qs_):
                        for q in qs_:
                            sl = slice(BATCH * q, BATCH * (q + 1))
                            act.wait_ge(s_dot, N * NQ + q + 1)
                            act.activation(acts[:, y, sl], dots[:, y, sl], ACT.Gelu_apprx_tanh).then_inc(s_act, 1)

                    def late_high(i):
                        if i < LATE:
                            act.wait_ge(s_late, 16 * (i + 1))
                            if i:
                                act.wait_ge(s_latefull, i)
                            else:
                                act.wait_ge(s_xr, NB)
                            act.activation(late_hi, late_raw, ACT.Copy).then_inc(s_latehi, 1)

                    def late_out(i):
                        if i < LATE:
                            act.wait_ge(s_latefull, i + 1)
                            act.activation(qT[:, :, EARLY + i], ps_q[i % 2].rearrange("p (b t) -> p b t", b=NB),
                                           ACT.Copy).then_inc(s_latefree, 1)

                    def residual(b):
                        act.wait_ge(s_free, l * SLOTS + (l * NB + b) * (PH * TOPK) + PH * TOPK + SLOTS)
                        for half in range(2):
                            act.activation(X[:, b, half * S:(half + 1) * S], ps_v[half], ACT.Copy).then_inc(s_vfree, 1)

                    for n in range(PH):
                        y, N = n % 2, l * NSEL + n
                        late_high(2 * n)
                        if EARLY // 2 <= n + 2 < PH:
                            act.wait_ge(s_latefree, 2 * (n + 2) - EARLY + 2)
                        stage(n + 2, y, sel0 + n + 1)
                        gelus(N, y, range(NQ // 2))
                        late_out(2 * n)
                        late_high(2 * n + 1)
                        gelus(N, y, range(NQ // 2, NQ))
                        late_out(2 * n + 1)
                        exps(sel0 + n + 3)
                    residual(0)
                    with act.Fori(1, NB) as b:
                        with act.Fori(0, PH // 2) as hp:
                            for y in range(2):
                                n, N = numbers(b, hp, y)
                                stage((n + 2) % NSEL, y, sel0 + n + 1)
                                gelus(N, y, range(NQ))
                                exps(sel0 + n + 3)
                        residual(b)

                @block.vector
                def _(dve):
                    own = Own(dve)

                    def rstd(ss, n):
                        dve.wait_ge(s_std, n)
                        own.link(dve.reciprocal(ss, ss), s_rstd)

                    def rstd_diagonal(ss, n):
                        rstd(ss, n)
                        dve.tensor_tensor(rdiag, ident.unsqueeze(1).to_broadcast([P, NB, P]),
                                          ss.unsqueeze(2).to_broadcast([P, NB, P]), ALU.mult).then_inc(s_rdiag, 1)

                    def lows(pair, gain, s_hi):
                        for k in range(NK):
                            dve.wait_ge(s_hi, k + 1)
                            dve.scalar_tensor_tensor(pair[1][:, k], ps[k], prm[:, gain + k:gain + k + 1],
                                                     pair[0][:, k].bitcast(F32), ALU.mult, ALU.subtract)\
                               .then_inc(s_tlow, 1)

                    for b in range(NB // 2, NB):
                        dve.tensor_tensor_reduce(h_rows[:, b], X[:, b], X[:, b], 1.0, 0.0, ALU.mult, ALU.add,
                                                 ss1[:, b:b + 1]).then_inc(s_sqd, 1)
                    rstd_diagonal(ss1, 1)
                    dve.wait_ge(s_par, 64)
                    lows(hT, P_MIXG, s_hhi)
                    rstd(ss2, 2)
                    for b in range(NB):
                        dve.tensor_scalar(v_rows[:, b], v_rows[:, b], ss2[:, b:b + 1], None, ALU.mult)\
                           .then_inc(s_vs, 1)
                    dve.wait_ge(s_one, 2)
                    for j in range(NK):
                        is_drained(dve, "xm", j)
                        cw = prm[:, P_CW + CONV * j:P_CW + CONV * (j + 1)]
                        own.link(dve.tensor_scalar(xcT[:, j], xmT[:, j, 0:S], cw[:, 0:1],
                                                   prm[:, P_CB + j:P_CB + j + 1], ALU.mult, ALU.add), s_d)
                        for w in range(1, CONV):
                            ins = dve.scalar_tensor_tensor(xcT[:, j], xmT[:, j, w:w + S], cw[:, w:w + 1],
                                                           xcT[:, j], ALU.mult, ALU.add)
                            if w < CONV - 1:
                                own.link(ins, s_d)
                            else:
                                ins.then_inc(s_conv, 1)
                    for g in range(NK):
                        z = is_filled(dve, "mix", g)
                        if g:
                            dve.wait_ge(s_ya, g)
                        t3 = tmp.rearrange("p (b t) -> p b t", b=NB)
                        drain(dve.scalar_tensor_tensor(t3, z.rearrange("p (b t) -> p b t", b=NB),
                                                       prm[:, P_GMG + g:P_GMG + g + 1],
                                                       bsb[:, g].unsqueeze(1).to_broadcast([P, NB, P]),
                                                       ALU.mult, ALU.add), "mix", g)
                        is_drained(dve, "mix", g)
                        is_drained(dve, "u", g)
                        dve.tensor_tensor(uT[:, g], tmp, uT[:, g], ALU.mult).then_inc(s_ya, 1)
                    for j in range(NK):
                        dve.wait_ge(s_sg, j + 1)
                        dve.tensor_tensor(xcT[:, j], xcT[:, j], sg, ALU.mult).then_inc(s_xc, 1)
                    is_drained(dve, "gates", 0)
                    dve.wait_ge(s_gin, 3)
                    dve.scalar_tensor_tensor(g_t, g_f, -1.0, g_f, ALU.mult, ALU.min).then_inc(s_nabs, 1)
                    dve.wait_ge(s_ln, 1)
                    own.link(dve.scalar_tensor_tensor(g_f, g_f, 0.0, g_t, ALU.min, ALU.subtract), s_d)
                    way = (slice(None), slice(None, None, -1))
                    for d in range(2):
                        own.link(dve.tensor_tensor_scan(g_F[:, d, way[d]], g_f[:, d, way[d]], g_f[:, d, way[d]],
                                                        0.0, ALU.add, ALU.bypass), s_d)
                    own.link(dve.tensor_tensor(g_i, g_i, g_F, ALU.subtract), s_d)
                    for d in range(2):
                        own.link(dve.tensor_tensor_scan(g_M[:, d, way[d]], g_i[:, d, way[d]], g_i[:, d, way[d]],
                                                        0.0, ALU.max, ALU.max), s_d)
                    dve.tensor_tensor(g_t, g_F, g_M, ALU.add).then_inc(s_fm, 1)
                    dve.tensor_scalar(g_f, g_M, -1.0, None, ALU.mult).then_inc(s_rows, 1)

                    def branch_a(j):
                        drain(dve.tensor_tensor(gaT[:, j], is_filled(dve, "a", j), gaT[:, j], ALU.mult), "a", j)

                    def head_out(f):
                        dve.wait_ge(s_hdfull, f + 1)
                        dve.wait_ge(s_xs, f + 1)
                        own.link(dve.scalar_tensor_tensor(xcT[:, f], ps_a[f % 2], prm[:, P_HG + f:P_HG + f + 1],
                                                          xcT[:, f], ALU.mult, ALU.add), s_hdout)
                        own.link(dve.tensor_tensor(xcT[:, f], oT[:, f], xcT[:, f], ALU.mult), s_ybval)
                        own.link(dve.tensor_copy(ybT[0][:, f], xcT[:, f]), s_ybhi)
                        dve.tensor_tensor(ybT[1][:, f], xcT[:, f], ybT[0][:, f].bitcast(F32), ALU.subtract)\
                           .then_inc(s_yb, 1)

                    branch_a(0)
                    branch_a(1)
                    z = is_filled(dve, "cols", 0)
                    drain(dve.tensor_copy(cols.rearrange("p i d b h -> p (i d b h)"), z[:, 0:64]), "cols", 0)
                    is_drained(dve, "cols", 0)

                    def arguments(h):
                        dve.wait_ge(s_afull, h + 1)
                        for c in range(NB):
                            for d in range(2):
                                w, t0, n = attn(d, c)
                                dve.tensor_scalar(w, ps_a[d][:, t0:t0 + n], cols[:, 0, d, c, h:h + 1], 0.0,
                                                  ALU.add, ALU.min).then_inc(s_arg, 1)

                    arguments(0)
                    for h in range(NH):
                        if h:
                            branch_a(2 * h)
                            branch_a(2 * h + 1)
                        for c in range(NB):
                            dve.wait_ge(s_sfull, NB * h + c + 1)
                            for d in range(2):
                                w, t0, n = attn(d, c)
                                dve.wait_ge(s_mask, 8 * h + 2 * c + d + 1)
                                dve.tensor_tensor(w, w, ps_s[c % 2][:, t0:t0 + n], ALU.mult).then_inc(s_p, 1)
                        if h and h < NH - 1:
                            head_out(2 * h - 2)
                            head_out(2 * h - 1)
                        for i in range(2 * NB):
                            d, b = i // NB, i % NB
                            dve.wait_ge(s_nfull, 8 * h + i + 1)
                            n_ = ps_n[i % 2]
                            own.link(dve.tensor_scalar(den[:, i:i + 1], n_[:, DH:VA], -1.0,
                                                       cols[:, 1, d, b, h:h + 1], ALU.mult, ALU.max), s_d)
                            own.link(dve.tensor_tensor(den[:, i:i + 1], den[:, i:i + 1], n_[:, DH:VA], ALU.max), s_d)
                            own.link(dve.reciprocal(den[:, i:i + 1], den[:, i:i + 1]), s_d)
                            if d == 0:
                                own.link(dve.tensor_scalar(h_head[:, b], n_[:, 0:DH], den[:, i:i + 1], None,
                                                           ALU.mult), s_nfree)
                            else:
                                dve.wait_ge(s_nfree, 4 * h + 4)
                                own.link(dve.scalar_tensor_tensor(h_head[:, b], n_[:, 0:DH], den[:, i:i + 1],
                                                                  h_head[:, b], ALU.mult, ALU.add), s_hsum)
                        if h + 1 < NH:
                            arguments(h + 1)
                        else:
                            head_out(2 * h - 2)
                            head_out(2 * h - 1)
                        rstd(hss, 3 + h)
                        dve.tensor_tensor(h_head, h_head, hss.unsqueeze(2).to_broadcast([P, NB, DH]),
                                          ALU.mult).then_inc(s_hn, 1)
                    head_out(2 * NH - 2)
                    head_out(2 * NH - 1)

                    def merged_lo(j):
                        dve.wait_ge(s_mhi, j + 1)
                        dve.tensor_tensor(mT[1][:, j], gaT[:, j], mT[0][:, j].bitcast(F32), ALU.subtract)\
                           .then_inc(s_ya, 1)

                    for j in range(NK):
                        drain(dve.tensor_tensor(gbT[:, j], is_filled(dve, "b", j), gbT[:, j], ALU.mult), "b", j)
                        is_drained(dve, "b", j)
                        own.link(dve.tensor_tensor(gaT[:, j], gaT[:, j], gbT[:, j], ALU.add), s_mval)
                        if j:
                            merged_lo(j - 1)
                    merged_lo(NK - 1)
                    for i in range(2 * NB):
                        half, b = i // NB, i % NB
                        xs = X[:, b, half * S:(half + 1) * S]
                        dve.wait_ge(s_wosum, i + 1)
                        dve.tensor_tensor(xs, xs, ps[4 + b], ALU.add).then_inc(s_wofree, 1)
                    dve.wait_ge(s_sqx, 2 * NB)
                    dve.tensor_tensor(ss3, ss3, ss5, ALU.add).then_inc(s_sqsum, 1)
                    rstd_diagonal(ss3, 3 + NH)
                    lows(xnT, P_FFG, s_xhi)
                    dve.wait_ge(s_ffg, 16)
                    for b in range(NB):
                        dve.scalar_tensor_tensor(xn[:, b], X[:, b], ss3[:, b:b + 1], ffg, ALU.mult, ALU.mult)\
                           .then_inc(s_xr, 1)

                    def step(ins):
                        own.link(ins, s_ps)

                    def top16(values, rest, best, where):
                        step(dve.max(best[:, 0:8], values))
                        step(dve.max_index(where[:, 0:8], best[:, 0:8], values))
                        step(dve.match_replace(rest, best[:, 0:8], values, LOWEST))
                        step(dve.max(best[:, 8:16], rest))
                        step(dve.max_index(where[:, 8:16], best[:, 8:16], rest))

                    def choose_first(y, scored):
                        dve.wait_ge(s_sc, scored)
                        step(dve.tensor_copy(sc2.rearrange("p h k -> p (h k)"), ps_k[y][:, 0:2 * KEYS]))
                        top16(sc2[:, 0], sc2r, sv[:, 0], si[:, 0])

                    def choose_second():
                        top16(sc2[:, 1], sc2r, sv[:, 1], si[:, 1])
                        step(dve.tensor_tensor(cand.rearrange("p (i j) -> p i j", i=TOPK),
                                               sv[:, 0].unsqueeze(2).to_broadcast([P, TOPK, TOPK]),
                                               sv[:, 1].unsqueeze(1).to_broadcast([P, TOPK, TOPK]), ALU.add))

                    def choose_pairs():
                        top16(cand, cand2, cv, ci)
                        dve.tensor_scalar(ncv, cv[:, 0:1], -1.0, None, ALU.mult).then_inc(s_cv, 1)

                    def find_rows(y):
                        step(dve.tensor_scalar(cab[:, 0], ci, 4, None, ALU.logical_shift_right))
                        step(dve.tensor_scalar(cab[:, 1], ci, TOPK - 1, None, ALU.bitwise_and))
                        full4 = [P, 2, TOPK, TOPK]
                        for h in range(2):
                            step(dve.tensor_tensor(onehot[:, h], iota16.unsqueeze(1).to_broadcast(full4[:1] + full4[2:]),
                                                   cab[:, h].unsqueeze(2).to_broadcast(full4[:1] + full4[2:]),
                                                   ALU.is_equal))
                        step(dve.tensor_tensor(picked, onehot, si.unsqueeze(2).to_broadcast(full4), ALU.mult))
                        step(dve.tensor_reduce(pick.rearrange("p h k -> p (h k)"),
                                               picked.rearrange("p h k j -> p (h k) j"), AX.X, ALU.add))
                        step(dve.tensor_scalar(pick[:, 0], pick[:, 0], float(KEYS), row0, ALU.mult, ALU.add))
                        dve.tensor_tensor(idx[:, y], pick[:, 0], pick[:, 1], ALU.add).then_inc(s_idx, 1)

                    def set_gate(y, exped):
                        dve.wait_ge(s_ex, exped)
                        step(dve.tensor_copy(rin, esum))
                        step(dve.reciprocal(rin, rin))
                        step(dve.tensor_scalar(gate[:, y], ex, rin, None, ALU.mult))

                    def next_round():
                        own.done(s_ps)
                        dve.sem_clear(s_ps)
                        own.forget(s_ps)

                    sel0 = l * (NSEL + 2)
                    choose_first(0, sel0 + 1)
                    choose_second()
                    choose_pairs()
                    find_rows(0)
                    set_gate(0, sel0 + 1)
                    choose_first(1, sel0 + 2)
                    choose_second()
                    choose_pairs()
                    next_round()
                    dve.wait_ge(s_xr, NB)
                    with dve.Fori(0, NB) as b:
                        step(dve.tensor_copy(x_now, xn[:, b]))
                        next_round()
                        with dve.Fori(0, PH // 2) as hp:
                            for y in range(2):
                                n, N = numbers(b, hp, y)
                                for q in range(NQ):
                                    sl = slice(BATCH * q, BATCH * (q + 1))
                                    for k in range(BATCH * q, BATCH * (q + 1)):
                                        r = k % SLOTS
                                        dve.wait_ge(s_gather[r], N * 32 + 16 * (k // SLOTS) + 16)
                                        ins = dve.tensor_tensor_reduce(slot[:, r, 0], slot[:, r, 0], x_now, 1.0, 0.0,
                                                                       ALU.mult, ALU.add, dots[:, y, k:k + 1])
                                    ins.then_inc(s_dot, 1)
                                    dve.wait_ge(s_act, N * NQ + q + 1)
                                    step(dve.tensor_tensor(wt[:, y, sl], acts[:, y, sl], gate[:, y, sl], ALU.mult))
                                    dve.wait_ge(s_free, l * SLOTS + N * TOPK + BATCH * (q + 1))
                                    r = BATCH * q % SLOTS
                                    dve.tensor_tensor(diag[:, r:r + BATCH],
                                                      ident.unsqueeze(1).to_broadcast([P, BATCH, P]),
                                                      wt[:, y, sl].unsqueeze(2).to_broadcast([P, BATCH, P]),
                                                      ALU.mult).then_inc(s_diag, 1)
                                    if q == 1:
                                        find_rows(1 - y)
                                    elif q == 3:
                                        set_gate(1 - y, sel0 + n + 2)
                                        choose_first(y, sel0 + n + 3)
                                    elif q == 5:
                                        choose_second()
                                    elif q == 7:
                                        choose_pairs()
                            next_round()
                    step(dve.tensor_scalar(row0, row0, float(KEYS * KEYS), None, ALU.add))
                    next_round()


                @block.tensor
                def _(pe):
                    pe.wait_ge(s_pool, 5)

                    def fill(*name):
                        n = FILL_NO[name]
                        if n >= 2:
                            pe.wait_ge(drained[n % 2], n // 2)
                        return bank[n % 2]

                    def full(ins, *name):
                        ins.then_inc(filled[FILL_NO[name] % 2], 1)

                    def parts(*name):
                        m = SPLIT_NO[name]
                        pe.wait_ge(s_wlo, m + 1)
                        return w_hi[:, m % PARTS], w_lo[:, m % PARTS]

                    def product(kind, j, x, ks=range(NK), ready=None):
                        z = fill(kind, j)
                        wh, wl = (w.rearrange("p (k c) -> p k c", k=NK) for w in parts(kind, j))
                        for k in ks:
                            if ready:
                                pe.wait_ge(ready[0], ready[1] + k + 1)
                            pe.matmul(z, wh[:, k], x[0][:, k], start=(k == 0), stop=False)
                            pe.matmul(z, wh[:, k], x[1][:, k], start=False, stop=False)
                            ins = pe.matmul(z, wl[:, k], x[0][:, k], start=False, stop=(k == NK - 1))
                        if ks[-1] == NK - 1:
                            full(ins, kind, j)

                    def product_a(j):
                        z, w = fill("a", j), loaded(pe, ("a", j)).rearrange("p (k c) -> p k c", k=NK)
                        for k in range(NK):
                            ins = pe.matmul(z, w[:, k], uT[:, k], start=(k == 0), stop=(k == NK - 1))
                        full(ins, "a", j)

                    def product_by_rows(kind, x, bank_of, before, tile_used, summed):
                        for j in range(NK):
                            half, m = j // 4, j % 4
                            wh, wl = (w.rearrange("p (k c) -> p k c", k=2) for w in parts(kind, j))
                            for b in range(NB):
                                before(half, m, b)
                                z = bank_of(half, b)
                                for i in range(2):
                                    k = 2 * m + i
                                    xh, xl = (t[:, k, b * P:(b + 1) * P] for t in x)
                                    end = m == 3 and i == 1
                                    pe.matmul(z, xh, wh[:, i], start=(m == 0 and i == 0), stop=False)
                                    pe.matmul(z, xh, wl[:, i], start=False, stop=False)
                                    ins = pe.matmul(z, xl, wh[:, i], start=False, stop=end)
                                if m == 3:
                                    ins.then_inc(summed, 1)
                            if m < 3:
                                ins.then_inc(tile_used, 1)

                    def turn_normed():
                        for k in range(NK):
                            for b in range(NB):
                                ins = pe.matmul(ps[k][:, b * P:(b + 1) * P], X[:, b, k * P:(k + 1) * P], rdiag[:, b],
                                                start=True, stop=True)
                            ins.then_inc(s_tfull, 1)

                    pe.wait_ge(s_rdiag, 1)
                    turn_normed()

                    def before_v(half, m, b):
                        if half == 0 and b == 0:
                            pe.wait_ge(s_tlow, max(2 * (m + 1), NB))

                    product_by_rows("v", hT, lambda half, b: ps[4 * half + b], before_v, s_vtile, s_vsum)
                    pe.wait_ge(s_vout, NB)
                    for kind in ("xm", "u"):
                        for j in range(NK):
                            product(kind, j, hT)
                    pe.wait_ge(s_vs, NB)
                    pe.wait_ge(s_par, 64)
                    for g in range(NK):
                        product("o", g, hT)
                        z = fill("mix", g)
                        for b in range(NB):
                            ins = pe.matmul(z[:, b * P:(b + 1) * P], v_rows[:, b, g * P:(g + 1) * P], wsT[:, g],
                                            start=True, stop=True)
                        full(ins, "mix", g)
                    for kind in ("ga", "gb"):
                        for j in range(NK):
                            product(kind, j, hT)
                    pe.wait_ge(s_xc, NK)
                    z = fill("gates", 0)
                    for k in range(NK):
                        ins = pe.matmul(z, wg[:, k], xcT[:, k], start=(k == 0), stop=(k == NK - 1))
                    full(ins, "gates", 0)

                    def qkv(h):
                        pe.wait_ge(s_qkvw, 16 * (h + 1))
                        for m, (w, dst) in enumerate((("q", qs), ("k", ks))):
                            for e in range(2):
                                z = fill(f"{w}{e}", h)
                                for c in range(2):
                                    ins = pe.matmul(z[:, :], WQKV[:, m, c, e * P:(e + 1) * P], xcT[:, 2 * h + c],
                                                    start=(c == 0), stop=(c == 1))
                                full(ins, f"{w}{e}", h)
                        for i in range(2):
                            z = fill(f"v{i}", h)
                            for b in range(2):
                                t0 = 2 + (2 * i + b) * P
                                for c in range(2):
                                    ins = pe.matmul(z[:, b * DH:(b + 1) * DH], xmT[:, 2 * h + c, t0:t0 + P],
                                                    WQKV[:, 2, c, :], start=(c == 0), stop=(c == 1))
                            full(ins, f"v{i}", h)

                    def head_turned(h):
                        pe.wait_ge(s_hn, h + 1)
                        if h == NH - 1:
                            pe.wait_ge(s_hdout, 2 * h)
                        pe.wait_ge(s_arg, 8 * min(h + 2, NH))
                        for e in range(2):
                            for b in range(NB):
                                ins = pe.transpose(ps_a[e][:, b * P:(b + 1) * P], h_head[:, b, e * P:(e + 1) * P],
                                                   ident)
                            ins.then_inc(s_hdfull, 1)

                    def stabilisers(h):
                        if h >= 2:
                            pe.wait_ge(s_hdout, 2 * (h - 1))
                        elif h:
                            pe.wait_ge(s_arg, 8 * h)
                        for d in range(2):
                            ins = pe.matmul(ps_a[d][:, :], sel[0:NH, h], g_f[:, d], start=True, stop=True)
                        ins.then_inc(s_afull, 1)

                    qkv(0)
                    pe.wait_ge(s_ya, NK)
                    product_a(0)
                    product_a(1)
                    z = fill("cols", 0)
                    pe.wait_ge(s_rows, 1)
                    pe.wait_ge(s_em, 1)
                    for i, g in enumerate((g_i, g_t)):
                        for d in range(2):
                            for b in range(NB):
                                o = ((i * 2 + d) * NB + b) * NH
                                ins = pe.transpose(z[:, o:o + NH], g[:, d, b * P:(b + 1) * P], ident[0:NH, 0:NH])
                    full(ins, "cols", 0)
                    pe.wait_ge(s_one, 4)
                    stabilisers(0)
                    for h in range(NH):
                        for n in ("q0", "q1", "k0", "k1", "v0", "v1"):
                            is_drained(pe, n, h)
                        for c in range(NB):
                            i = NB * h + c
                            if i >= 2:
                                pe.wait_ge(s_p, 2 * (i - 1))
                            for e in range(2):
                                ins = pe.matmul(ps_s[c % 2][:, :], ks[:, e, c * P:(c + 1) * P], qs[:, e],
                                                start=(e == 0), stop=(e == 1))
                            ins.then_inc(s_sfull, 1)
                        if h:
                            head_turned(h - 1)
                        if h + 1 < NH:
                            qkv(h + 1)
                        pe.wait_ge(s_p, 8 * (h + 1))
                        for i in range(2 * NB):
                            d, b = i // NB, i % NB
                            if i in (0, 1):
                                if h:
                                    pe.wait_ge(s_hsum, 4 * h - 1 + i)
                            elif i < 6:
                                pe.wait_ge(s_nfree, 4 * h + i - 1)
                            else:
                                pe.wait_ge(s_hsum, 4 * h + i - 5)
                            srcs = range(0, b + 1) if d == 0 else range(b, NB)
                            for c in srcs:
                                w, t0, n = attn(d, c)
                                ins = pe.matmul(ps_n[i % 2][:, 0:VA], w[:, b * P - t0:(b + 1) * P - t0],
                                                vaug[h % 2][:, c], start=(c == srcs[0]), stop=(c == srcs[-1]))
                            ins.then_inc(s_nfull, 1)
                        if h + 1 < NH:
                            stabilisers(h + 1)
                            product_a(2 * h + 2)
                            product_a(2 * h + 3)
                    for j in range(2):
                        product("b", j, ybT, range(NK - 2), (s_yb, 0))
                    head_turned(NH - 1)
                    for j in range(2):
                        product("b", j, ybT, range(NK - 2, NK), (s_yb, 0))
                    for j in range(2, NK):
                        product("b", j, ybT)

                    def before_wo(half, m, b):
                        if half == 0 and b == 0:
                            pe.wait_ge(s_ya, NK + 2 * (m + 1))
                        if half and m == 0:
                            pe.wait_ge(s_wofree, b + 1)

                    product_by_rows("wo", mT, lambda half, b: ps[4 + b], before_wo, s_wotile, s_wosum)
                    pe.wait_ge(s_rdiag, 2)
                    turn_normed()
                    pe.sem_inc(s_free, SLOTS // 2)

                    sel0 = l * (NSEL + 2)

                    def key_scores(y, head, staged, copied):
                        if copied is not None:
                            pe.wait_ge(s_cv, copied)
                        pe.wait_ge(s_q, staged)
                        for h in range(2):
                            ins = pe.matmul(ps_k[y][:, h * KEYS:(h + 1) * KEYS], q_now[:, y, h],
                                            keysT[:, head * 2 + h], start=True, stop=True)
                        ins.then_inc(s_sc, 1)

                    pe.wait_ge(s_keys, 16)
                    for j in range(EARLY):
                        product("pq", j, xnT, ready=(s_tlow, NK) if j == 0 else None)
                        if j in SCORES_AT:
                            m = SCORES_AT.index(j)
                            key_scores(m, m, sel0 + m + 1, None)
                    is_drained(pe, "pq", EARLY - 2)
                    is_drained(pe, "pq", EARLY - 1)
                    pe.sem_inc(s_free, SLOTS // 2)

                    def start_sum(b):
                        pe.wait_ge(s_vfree, 2 * (l * NB + b) + 2)
                        for half in range(2):
                            pe.matmul(ps_v[half], ident, X[:, b, half * S:(half + 1) * S], start=True, stop=False,
                                      skip_group_check=True)

                    def weighted(N, q):
                        pe.wait_ge(s_diag, N * NQ + q + 1)
                        for k in range(BATCH):
                            r = (BATCH * q + k) % SLOTS
                            for half in range(2):
                                ins = pe.matmul(ps_v[half], diag[:, r], slot[:, r, 1, half * S:(half + 1) * S],
                                                start=False, stop=False, skip_group_check=True)
                            ins.then_inc(s_free, 1)

                    def late_product(i):
                        if i < LATE:
                            if i >= 2:
                                pe.wait_ge(s_latefree, i - 1)
                            pe.wait_ge(s_latelo, i + 1)
                            wh, wl = (w.rearrange("p (k c) -> p k c", k=NK) for w in (late_hi, late_lo))
                            for k in range(NK):
                                pe.matmul(ps_q[i % 2], wh[:, k], xnT[0][:, k], start=(k == 0), stop=False)
                                pe.matmul(ps_q[i % 2], wh[:, k], xnT[1][:, k], start=False, stop=False)
                                ins = pe.matmul(ps_q[i % 2], wl[:, k], xnT[0][:, k], start=False, stop=(k == NK - 1))
                            ins.then_inc(s_latefull, 1)

                    start_sum(0)
                    for n in range(PH):
                        N = l * NSEL + n
                        key_scores(n % 2, (n + 2) % PH, sel0 + n + 3, sel0 + n + 1)
                        for q in range(NQ):
                            weighted(N, q)
                            if q == 1:
                                late_product(2 * n)
                            elif q == 5:
                                late_product(2 * n + 1)
                    with pe.Fori(1, NB) as b:
                        start_sum(b)
                        with pe.Fori(0, PH // 2) as hp:
                            for y in range(2):
                                n, N = numbers(b, hp, y)
                                key_scores(y, (hp * 2 + y + 2) % PH, sel0 + n + 3, sel0 + n + 1)
                                for q in range(NQ):
                                    weighted(N, q)

            nc.all_engine_barrier()
            with nc.Block() as block:
                @block.sync
                def _(sp):
                    lo, hi = filled[0].num, s_clear_last.num
                    sp.sem_clear(range(lo, hi + 1))

        with nc.Block() as block:
            @block.sync
            def _(sp):
                sp.dma_start(ffg, fin_g.to_broadcast([P, D])).then_inc(s_x, 16)
                for b in range(NB):
                    sp.wait_ge(s_fin, b + 1)
                    sp.dma_start(out[b * P:(b + 1) * P, :], xn[:, b]).then_inc(s_out, 16)
                sp.wait_ge(s_out, 16 * NB)

            @block.scalar
            def _(act):
                for b in range(NB):
                    act.activation(h_rows[:, b], X[:, b], ACT.Square, accum_out=ss4[:, b:b + 1]).then_inc(s_fsq, 1)
                    act.wait_ge(s_fsq, b + 1)
                    act.activation(ss4[:, b:b + 1], ss4[:, b:b + 1], ACT.Sqrt, bias=eps, scale=1.0 / D)\
                       .then_inc(s_fstd, 1)

            @block.vector
            def _(dve):
                for b in range(NB):
                    dve.wait_ge(s_fstd, b + 1)
                    dve.reciprocal(ss4[:, b:b + 1], ss4[:, b:b + 1]).then_inc(s_frs, 1)
                    dve.wait_ge(s_frs, b + 1)
                    if b == 0:
                        dve.wait_ge(s_x, 32)
                    dve.scalar_tensor_tensor(xn[:, b], X[:, b], ss4[:, b:b + 1], ffg, ALU.mult, ALU.mult)\
                       .then_inc(s_fin, 1)


_PARAMS = ("norm_mix_g", "gm_norm_g", "ml_conv_b", "ml_head_g", "ml_skip", "norm_ffn_g")


def _launch_arrays(i):
    import numpy as np

    a = {k: np.asarray(v) for k, v in i.items()}
    f = np.float32

    def by_feature(v):
        return v.reshape(L, NK, P).transpose(0, 2, 1)

    def by_tile(w):
        n = w.shape[2] // P
        return w.reshape(L, NK, P, n, P).transpose(0, 3, 2, 1, 4)

    def by_half(w):
        return w.reshape(L, 4, 2, P, 2, S).transpose(0, 4, 1, 3, 2, 5).reshape(L, 8, P, NK, P)

    w_in = a["w_in"]
    par = np.zeros((L, P, NPAR), f)
    for n, name in enumerate(_PARAMS):
        par[:, :, 8 * n:8 * n + 8] = by_feature(a[name].reshape(L, D))
    cw = a["ml_conv_w"].reshape(L, CONV, NK, P).transpose(0, 3, 2, 1)
    par[:, :, P_CW:P_BG] = cw.reshape(L, P, NK * CONV)
    par[:, 0:NH, P_BG:] = a["ml_b_gate"].reshape(L, 4, NH).transpose(0, 2, 1)
    wg = np.zeros((L, D, P), f)
    for t in range(4):
        wg[:, :, 32 * t:32 * t + NH] = a["ml_w_gate"][:, :, NH * t:NH * (t + 1)]
    qkv = np.stack([a[n].reshape(L, NH, 2, P, DH) for n in ("ml_w_q", "ml_w_k", "ml_w_v")], axis=3)
    out = {
        "x_in": a["x"].reshape(S, D),
        "par": par,
        "bs": a["gm_b_s"],
        "ws": a["gm_w_s"].transpose(0, 3, 1, 2),
        "w_in": by_tile(np.concatenate([w_in[:, :, :D], w_in[:, :, 2 * D:]], axis=2)),
        "w_qkv": qkv.transpose(0, 1, 4, 3, 2, 5),
        "w_g": wg.reshape(L, NK, P, P).transpose(0, 2, 1, 3),
        "w_a": by_tile(a["w_branch_a"]),
        "w_b": by_tile(a["w_branch_b"]),
        "w_v": by_half(w_in[:, :, D:2 * D]),
        "w_o": by_half(a["w_out"]),
        "ffn_g": a["norm_ffn_g"],
        "w_pq": by_tile(a["peer_w_query"]),
        "keys": a["peer_sub_keys"].reshape(L, 2 * PH, KEYS, P).transpose(0, 3, 1, 2),
        "uv": np.concatenate([a["peer_u"], a["peer_v"]], axis=2).reshape(L * KEYS * KEYS, 2 * D),
        "fin_g": a["final_g"].reshape(1, D),
    }
    return {k: np.ascontiguousarray(v) for k, v in out.items()}


def kernel(**inputs):
    import concourse.bacc as bacc
    from concourse.bass_utils import run_bass_kernel_spmd as run

    nc = bacc.Bacc("TRN2", target_bir_lowering=False, num_devices=1)
    arrays = _launch_arrays(inputs)
    aps = {n: nc.dram_tensor(f"in_{n}", v.shape, mybir.dt.from_np(v.dtype), kind="ExternalInput").ap()
           for n, v in arrays.items()}
    out = nc.dram_tensor("out", (S, D), F32, kind="ExternalOutput").ap()
    build(nc, out=out, **aps)
    r = run(nc, [{f"in_{n}": v for n, v in arrays.items()}], core_ids=[0])
    return r.results[0]["out"].reshape(1, S, D)
```
